# Optimizing a Trainium2 kernel written in Bass

```python
import math
import jax, jax.numpy as jnp
from jax import lax
import numpy as np

D_MODEL = 1024
BATCH = 1
SEQ = 1024
DEPTH = 1
DEC_BATCH = 8
DEC_SEQ = 8
PAST_LEN = 1024
PAGE_SIZE = 128

D_ATTN = D_MODEL // 2
D_SSM = D_MODEL - D_ATTN
H_A = 4
DV = D_ATTN // H_A
DQK = DV // 2
Q_BLOCK = 128
SSM_CH = 16
SSM_GROUPS = D_SSM // SSM_CH
SSM_P = 64
PEER_HEADS = 8
PEER_KEYS = 128
PEER_EXPERTS = PEER_KEYS * PEER_KEYS
PEER_TOPK = 16
PEER_DKEY = 256
PEER_DHALF = PEER_DKEY // 2
PEER_BLOCK = 128
ALPHA = (2.0 * DEPTH) ** 0.25
BETA = (8.0 * DEPTH) ** -0.25
EPS = 1e-5
MASK_VALUE = -1e30

kernel_name = "hymba_diffattn_s5_peer_step"

def layer_norm(x, g, b):
    xf = x.astype(jnp.float32)
    mu = jnp.mean(xf, axis=-1, keepdims=True)
    var = jnp.mean(jnp.square(xf - mu), axis=-1, keepdims=True)
    return ((xf - mu) * lax.rsqrt(var + EPS) * g.astype(jnp.float32) + b.astype(jnp.float32)).astype(x.dtype)

def rms_norm(x, g):
    xf = x.astype(jnp.float32)
    return (xf * lax.rsqrt(jnp.mean(xf * xf, axis=-1, keepdims=True) + EPS) * g.astype(jnp.float32)).astype(x.dtype)

def alibi_slopes():
    return 2.0 ** (-8.0 * jnp.arange(1, H_A + 1, dtype=jnp.float32) / H_A)

def project(x, w_in):
    b, t = x.shape[:2]
    z = x @ w_in
    q = z[..., :D_ATTN].reshape(b, t, H_A, 2, DQK)
    k = z[..., D_ATTN:2 * D_ATTN].reshape(b, t, H_A, 2, DQK)
    v = z[..., 2 * D_ATTN:3 * D_ATTN].reshape(b, t, H_A, DV)
    u = z[..., 3 * D_ATTN:]
    return q, k, v, u

def diff_attention(q, k, v, q_pos, k_pos, lam, subln_g, lam_init):
    s = jnp.einsum('bqhcd,bkhcd->bhcqk', q, k).astype(jnp.float32) * (DQK ** -0.5)
    dist = (q_pos[:, None] - k_pos[None, :]).astype(jnp.float32)
    bias = -alibi_slopes()[:, None, None] * jnp.abs(dist)
    causal = q_pos[:, None] >= k_pos[None, :]
    s = jnp.where(causal, s + bias[None, :, None], MASK_VALUE)
    p = jax.nn.softmax(s, axis=-1)
    a = p[:, :, 0] - lam * p[:, :, 1]
    o = jnp.einsum('bhqk,bkhd->bqhd', a.astype(v.dtype), v)
    o = rms_norm(o, subln_g) * (1.0 - lam_init)
    return o.reshape(o.shape[0], o.shape[1], D_ATTN)

def prompt_attention(q, k, v, lam, subln_g, lam_init):
    b, s = q.shape[:2]
    nb = s // Q_BLOCK
    qb = q.reshape(b, nb, Q_BLOCK, H_A, 2, DQK).transpose(1, 0, 2, 3, 4, 5)
    k_pos = jnp.arange(s, dtype=jnp.int32)

    def one_block(args):
        q_blk, blk = args
        q_pos = blk * Q_BLOCK + jnp.arange(Q_BLOCK, dtype=jnp.int32)
        return diff_attention(q_blk, k, v, q_pos, k_pos, lam, subln_g, lam_init)

    o = lax.map(one_block, (qb, jnp.arange(nb, dtype=jnp.int32)))
    return o.transpose(1, 0, 2, 3).reshape(b, s, D_ATTN)

def ssm_combine(e1, e2):
    ar1, ai1, br1, bi1 = e1
    ar2, ai2, br2, bi2 = e2
    return (ar2 * ar1 - ai2 * ai1, ar2 * ai1 + ai2 * ar1,
            ar2 * br1 - ai2 * bi1 + br2, ar2 * bi1 + ai2 * br1 + bi2)

def s5_mixer(u, h0_re, h0_im, lam_re, lam_im, log_dt, b_re, b_im, c_re, c_im, d_skip, w_glu, b_glu):
    f32 = jnp.float32
    bsz, t = u.shape[:2]
    uf = u.astype(f32).reshape(bsz, t, SSM_GROUPS, SSM_CH)
    lr, li = lam_re.astype(f32), lam_im.astype(f32)
    dt = jnp.exp(log_dt.astype(f32))[:, None]
    mag = jnp.exp(lr * dt)
    a_re, a_im = mag * jnp.cos(li * dt), mag * jnp.sin(li * dt)
    den = lr * lr + li * li
    n_re, n_im = a_re - 1.0, a_im
    g_re = (n_re * lr + n_im * li) / den
    g_im = (n_im * lr - n_re * li) / den
    br, bi = b_re.astype(f32), b_im.astype(f32)
    bb_re = g_re[..., None] * br - g_im[..., None] * bi
    bb_im = g_re[..., None] * bi + g_im[..., None] * br
    bu_re = jnp.einsum('btgc,gpc->btgp', uf, bb_re)
    bu_im = jnp.einsum('btgc,gpc->btgp', uf, bb_im)
    h0r, h0i = h0_re.astype(f32), h0_im.astype(f32)
    bu_re = bu_re.at[:, 0].add(a_re * h0r - a_im * h0i)
    bu_im = bu_im.at[:, 0].add(a_re * h0i + a_im * h0r)
    ar = jnp.broadcast_to(a_re, bu_re.shape)
    ai = jnp.broadcast_to(a_im, bu_im.shape)
    _, _, h_re, h_im = lax.associative_scan(ssm_combine, (ar, ai, bu_re, bu_im), axis=1)
    y = (jnp.einsum('gcp,btgp->btgc', c_re.astype(f32), h_re)
         - jnp.einsum('gcp,btgp->btgc', c_im.astype(f32), h_im)
         + d_skip.astype(f32) * uf)
    y = jax.nn.gelu(y.reshape(bsz, t, D_SSM), approximate=False)
    out = y * jax.nn.sigmoid(y @ w_glu.astype(f32) + b_glu.astype(f32))
    return out.astype(u.dtype), h_re[:, -1], h_im[:, -1]

def peer_block(x, w_q, q_g, sub_keys, u_tab, v_tab):
    t = x.shape[0]
    q = rms_norm((x @ w_q).reshape(t, PEER_HEADS, PEER_DKEY), q_g).reshape(t, PEER_HEADS, 2, PEER_DHALF)
    s = jnp.einsum('thcd,hcnd->thcn', q, sub_keys).astype(jnp.float32)
    s_top, i_top = lax.top_k(s, PEER_TOPK)
    cand = (s_top[:, :, 0, :, None] + s_top[:, :, 1, None, :]).reshape(t, PEER_HEADS, PEER_TOPK * PEER_TOPK)
    cand_idx = (i_top[:, :, 0, :, None] * PEER_KEYS + i_top[:, :, 1, None, :]).reshape(t, PEER_HEADS, PEER_TOPK * PEER_TOPK)
    best, pos = lax.top_k(cand, PEER_TOPK)
    idx = jnp.take_along_axis(cand_idx, pos, axis=-1)
    g = jax.nn.softmax(best, axis=-1)
    u = jnp.take(u_tab, idx, axis=0)
    act = jax.nn.gelu(jnp.einsum('thkd,td->thk', u, x).astype(jnp.float32), approximate=False)
    v = jnp.take(v_tab, idx, axis=0)
    return jnp.einsum('thk,thkd->td', (g * act).astype(x.dtype), v)

def peer_apply(x, w_q, q_g, sub_keys, u_tab, v_tab):
    b, t, d = x.shape
    n = b * t
    blk = PEER_BLOCK if n % PEER_BLOCK == 0 else n
    xb = x.reshape(n // blk, blk, d)
    out = lax.map(lambda xi: peer_block(xi, w_q, q_g, sub_keys, u_tab, v_tab), xb)
    return out.reshape(b, t, d)

def finish(x, a, s, w_out, ln1_g, ln1_b, peer_w_q, peer_q_g, peer_sub_keys, peer_u, peer_v, ln2_g, ln2_b):
    h = jnp.concatenate([a, s], axis=-1) @ w_out
    x1 = layer_norm(ALPHA * x + h, ln1_g, ln1_b)
    f = peer_apply(x1, peer_w_q, peer_q_g, peer_sub_keys, peer_u, peer_v)
    return layer_norm(ALPHA * x1 + f, ln2_g, ln2_b)

def setup_inputs(seed: int = 0) -> dict:
    key = jax.random.key(seed)
    ks = jax.random.split(key, 40)
    f32 = jnp.float32

    def nrm(k, shape, scale):
        return jax.random.normal(k, shape, f32) * scale

    n_pages = PAST_LEN // PAGE_SIZE
    n_phys = (DEC_BATCH * n_pages * 5) // 4
    page_table = jax.random.permutation(ks[0], n_phys)[:DEC_BATCH * n_pages].reshape(DEC_BATCH, n_pages).astype(jnp.int32)
    ws = D_MODEL ** -0.5
    w_in = jnp.concatenate([
        nrm(ks[7], (DEPTH, D_MODEL, 2 * D_ATTN), ws),
        nrm(ks[8], (DEPTH, D_MODEL, D_ATTN), ws * BETA),
        nrm(ks[9], (DEPTH, D_MODEL, D_SSM), ws),
    ], axis=-1)
    lam_im0 = jnp.broadcast_to(jnp.pi * jnp.arange(SSM_P, dtype=f32), (DEPTH, SSM_GROUPS, SSM_P))
    return {
        "x_prompt": nrm(ks[1], (BATCH, SEQ, D_MODEL), 1.0),
        "x_sample": nrm(ks[2], (DEC_BATCH, DEC_SEQ, D_MODEL), 1.0),
        "cache_k": nrm(ks[3], (DEPTH, n_phys, PAGE_SIZE, H_A, 2, DQK), 1.0),
        "cache_v": nrm(ks[4], (DEPTH, n_phys, PAGE_SIZE, H_A, DV), BETA),
        "state_ssm_re": nrm(ks[5], (DEPTH, DEC_BATCH, SSM_GROUPS, SSM_P), 0.1),
        "state_ssm_im": nrm(ks[6], (DEPTH, DEC_BATCH, SSM_GROUPS, SSM_P), 0.1),
        "page_table": page_table,
        "w_in": w_in,
        "lambda_q1": nrm(ks[10], (DEPTH, DQK), 0.1),
        "lambda_k1": nrm(ks[11], (DEPTH, DQK), 0.1),
        "lambda_q2": nrm(ks[12], (DEPTH, DQK), 0.1),
        "lambda_k2": nrm(ks[13], (DEPTH, DQK), 0.1),
        "attn_subln_g": 1.0 + nrm(ks[14], (DEPTH, DV), 0.01),
        "ssm_lambda_re": -0.5 + nrm(ks[15], (DEPTH, SSM_GROUPS, SSM_P), 1e-3),
        "ssm_lambda_im": lam_im0 + nrm(ks[16], (DEPTH, SSM_GROUPS, SSM_P), 1e-3),
        "ssm_log_dt": jax.random.uniform(ks[17], (DEPTH, SSM_GROUPS), f32, math.log(1e-3), math.log(1e-1)),
        "ssm_b_re": nrm(ks[18], (DEPTH, SSM_GROUPS, SSM_P, SSM_CH), (2 * SSM_CH) ** -0.5),
        "ssm_b_im": nrm(ks[19], (DEPTH, SSM_GROUPS, SSM_P, SSM_CH), (2 * SSM_CH) ** -0.5),
        "ssm_c_re": nrm(ks[20], (DEPTH, SSM_GROUPS, SSM_CH, SSM_P), (2 * SSM_P) ** -0.5),
        "ssm_c_im": nrm(ks[21], (DEPTH, SSM_GROUPS, SSM_CH, SSM_P), (2 * SSM_P) ** -0.5),
        "ssm_d": nrm(ks[22], (DEPTH, SSM_GROUPS, SSM_CH), 1.0),
        "ssm_w_glu": nrm(ks[23], (DEPTH, D_SSM, D_SSM), D_SSM ** -0.5),
        "ssm_b_glu": nrm(ks[24], (DEPTH, D_SSM), 0.01),
        "w_out": nrm(ks[25], (DEPTH, D_MODEL, D_MODEL), ws * BETA),
        "ln1_g": 1.0 + nrm(ks[26], (DEPTH, D_MODEL), 0.01),
        "ln1_b": nrm(ks[27], (DEPTH, D_MODEL), 0.01),
        "peer_w_q": nrm(ks[28], (DEPTH, D_MODEL, PEER_HEADS * PEER_DKEY), ws),
        "peer_q_g": 1.0 + nrm(ks[29], (DEPTH, PEER_DKEY), 0.01),
        "peer_sub_keys": nrm(ks[30], (DEPTH, PEER_HEADS, 2, PEER_KEYS, PEER_DHALF), PEER_DHALF ** -0.5),
        "peer_u": nrm(ks[31], (DEPTH, PEER_EXPERTS, D_MODEL), ws),
        "peer_v": nrm(ks[32], (DEPTH, PEER_EXPERTS, D_MODEL), BETA),
        "ln2_g": 1.0 + nrm(ks[33], (DEPTH, D_MODEL), 0.01),
        "ln2_b": nrm(ks[34], (DEPTH, D_MODEL), 0.01),
    }

def reference(x_prompt, x_sample, cache_k, cache_v, state_ssm_re, state_ssm_im, page_table,
              w_in, lambda_q1, lambda_k1, lambda_q2, lambda_k2, attn_subln_g,
              ssm_lambda_re, ssm_lambda_im, ssm_log_dt, ssm_b_re, ssm_b_im, ssm_c_re, ssm_c_im,
              ssm_d, ssm_w_glu, ssm_b_glu, w_out, ln1_g, ln1_b,
              peer_w_q, peer_q_g, peer_sub_keys, peer_u, peer_v, ln2_g, ln2_b):
    f32 = jnp.float32
    n_pages = PAST_LEN // PAGE_SIZE
    sample_q_pos = PAST_LEN + jnp.arange(DEC_SEQ, dtype=jnp.int32)
    sample_k_pos = jnp.arange(PAST_LEN + DEC_SEQ, dtype=jnp.int32)
    zero_state = jnp.zeros((BATCH, SSM_GROUPS, SSM_P), f32)
    xp, xs = x_prompt, x_sample
    kp_rows, vp_rows, hpr, hpi = [], [], [], []
    ks_rows, vs_rows, hsr, hsi = [], [], [], []
    for l in range(DEPTH):
        lam_init = 0.8 - 0.6 * math.exp(-0.3 * l)
        lam = (jnp.exp(jnp.sum(lambda_q1[l].astype(f32) * lambda_k1[l].astype(f32)))
               - jnp.exp(jnp.sum(lambda_q2[l].astype(f32) * lambda_k2[l].astype(f32))) + lam_init)
        ssm_args = (ssm_lambda_re[l], ssm_lambda_im[l], ssm_log_dt[l], ssm_b_re[l], ssm_b_im[l],
                    ssm_c_re[l], ssm_c_im[l], ssm_d[l], ssm_w_glu[l], ssm_b_glu[l])
        tail_args = (w_out[l], ln1_g[l], ln1_b[l], peer_w_q[l], peer_q_g[l], peer_sub_keys[l],
                     peer_u[l], peer_v[l], ln2_g[l], ln2_b[l])

        qp, kp, vp, up = project(xp, w_in[l])
        ap = prompt_attention(qp, kp, vp, lam, attn_subln_g[l], lam_init)
        sp, h_re_p, h_im_p = s5_mixer(up, zero_state, zero_state, *ssm_args)
        xp = finish(xp, ap, sp, *tail_args)

        qs, kss, vss, us = project(xs, w_in[l])
        k_past = cache_k[l][page_table].reshape(DEC_BATCH, n_pages * PAGE_SIZE, H_A, 2, DQK)
        v_past = cache_v[l][page_table].reshape(DEC_BATCH, n_pages * PAGE_SIZE, H_A, DV)
        k_all = jnp.concatenate([k_past.astype(kss.dtype), kss], axis=1)
        v_all = jnp.concatenate([v_past.astype(vss.dtype), vss], axis=1)
        a_s = diff_attention(qs, k_all, v_all, sample_q_pos, sample_k_pos, lam, attn_subln_g[l], lam_init)
        s_s, h_re_s, h_im_s = s5_mixer(us, state_ssm_re[l], state_ssm_im[l], *ssm_args)
        xs = finish(xs, a_s, s_s, *tail_args)

        kp_rows.append(kp); vp_rows.append(vp); hpr.append(h_re_p); hpi.append(h_im_p)
        ks_rows.append(kss); vs_rows.append(vss); hsr.append(h_re_s); hsi.append(h_im_s)

    k_prompt = jnp.stack(kp_rows)
    v_prompt = jnp.stack(vp_rows)
    ssm_re_prompt = jnp.stack(hpr)
    ssm_im_prompt = jnp.stack(hpi)
    k_sample = jnp.stack(ks_rows)
    v_sample = jnp.stack(vs_rows)
    ssm_re_sample = jnp.stack(hsr)
    ssm_im_sample = jnp.stack(hsi)
    return (xp, xs, k_prompt, v_prompt, ssm_re_prompt, ssm_im_prompt,
            k_sample, v_sample, ssm_re_sample, ssm_im_sample)


_drawn_inputs = setup_inputs


def setup_inputs(seed=0):
    import zlib

    import numpy as np

    out = dict(_drawn_inputs(seed))
    spreads = {}
    factors = {'lambda_q1': 4.792,
     'attn_subln_g': 4.083,
     'ssm_lambda_re': 64.0,
     'ssm_b_glu': 30.145,
     'ln2_g': 32.225,
     'ln2_b': 32.37,
     'ssm_c_re': 2.943,
     'ssm_c_im': 2.78}
    for name, (base, spread) in spreads.items():
        noise = np.random.default_rng([zlib.crc32(name.encode()), seed]).standard_normal(out[name].shape)
        drawn = base * np.exp(spread * noise) if base else spread * noise
        out[name] = __import__('jax').numpy.asarray(drawn.astype(out[name].dtype))
    for name, factor in factors.items():
        out[name] = (out[name] * factor).astype(out[name].dtype)
    return out
```

```python
import math
from contextlib import ExitStack

import numpy as np
import concourse.bass as bass
from concourse import mybir
from concourse.alu_op_type import AluOpType as ALU

F32 = mybir.dt.float32
I32 = mybir.dt.int32
U32 = mybir.dt.uint32
ACT = mybir.ActivationFunctionType
X = mybir.AxisListType.X

P = 128
DM = 1024
KC = DM // P
SEQ = 1024
NT = SEQ // P
DB, DS = 8, 8
SR = DB * DS
TP = SEQ + P
DA = 512
H = 4
DQ = 64
DV = 128
G, C, SP_ = 32, 16, 64
GP = G // 2
L = 8
NCH = SEQ // L
NC = NCH + DB
PAST = 1024
PG = 8
EH = 8
TOP = 16
NK = EH * TOP
NKEY = 128
EPS = 1e-5
ALPHA = 2.0 ** 0.25
LAM_INIT = 0.8 - 0.6 * math.exp(0.0)
SLOPE = [2.0 ** (-8.0 * (h + 1) / H) for h in range(H)]
QSCALE = [DQ ** -0.5 / s for s in SLOPE]
MASKED = -1e34
LOW = -3.0e38
WB = SEQ - P
RING = 4
GR = 8

PI2A = 6.28125
PI2B = 0.0019350051879882812
PI2C = 2 * math.pi - PI2A - PI2B
MAGIC = 12582912.0


class Steps:

    def __init__(self, eng, sem):
        self.eng, self.sem, self.n = eng, sem, 0

    def __call__(self, ins):
        self.n += 1
        ins.then_inc(self.sem, 1)
        self.eng.wait_ge(self.sem, self.n)

    def restart(self):
        self.eng.sem_clear(self.sem)
        self.n = 0


def build(nc, a, o):
    top = ExitStack()
    with top:
        def alloc(ctx):
            def sb(name, shape, dt=F32):
                return ctx.enter_context(nc.sbuf_tensor(name, shape, dt))
            return sb

        sems = {}

        def sem(name):
            if name not in sems:
                sems[name] = top.enter_context(nc.semaphore(name))
            return sems[name]

        sb = alloc(top)
        ident = sb("ident", [P, P])
        zero = sb("zero", [P, 1])
        kT = sb("kT", [P, H, TP])
        vrows = sb("vrows", [P, NT + 1, DA])
        neglam = sb("neglam", [P, 1])
        psum = top.enter_context(nc.psum_tensor("psum", [P, 8, 512], F32))
        bank = [psum[:, i, :] for i in range(8)]

        scr_q = nc.dram_tensor("scr_q", (P, H, TP), F32, kind="Internal").ap()
        scr_s = nc.dram_tensor("scr_s", (P, H, TP), F32, kind="Internal").ap()
        scr_u = nc.dram_tensor("scr_u", (G, C, L, NC), F32, kind="Internal").ap()
        scr_y = nc.dram_tensor("scr_y", (G, C, L, NC), F32, kind="Internal").ap()

        projections(nc, a, o, alloc, sem, ident, zero, kT, vrows, neglam, bank, scr_q, scr_u)
        state_space(nc, a, o, alloc, sem, ident, bank, scr_u, scr_y, scr_s)
        trunk(nc, a, o, alloc, sem, ident, kT, vrows, neglam, bank, psum, scr_q, scr_s)


def projections(nc, a, o, alloc, sem, ident, zero, kT, vrows, neglam, bank, scr_q, scr_u):
    with ExitStack() as ctx:
        sb = alloc(ctx)
        w = sb("w_in_sb", [P, KC, 4 * DA])
        xr = sb("xr", [P, 2, DM])
        xT = sb("xT", [P, KC, P])
        qrow = sb("qrow", [P, DA])
        krow = sb("krow", [P, DA])
        urow = sb("urow", [P, DA])
        qTs = sb("qTs", [P, H, P])
        uT = sb("uT", [P, 4, L, TP // L])
        lamv = sb("lamv", [P, 4, DQ])
        lamw = sb("lamw", [P, DQ])
        lams = sb("lams", [P, 4])
        k_rows = o[2].rearrange("d b t h c q -> (d b t) (h c q)")
        v_rows = o[3].rearrange("d b t h v -> (d b t) (h v)")
        ks_rows = o[6].rearrange("d b t h c q -> (d b t) (h c q)")
        vs_rows = o[7].rearrange("d b t h v -> (d b t) (h v)")
        x_rows = a["x_all"]
        w_v = a["w_in"].rearrange("o (k p) n -> p (o k) n", p=P)

        with nc.Block() as block:

            @block.sync
            def _(sp):
                for n, name in enumerate(("lambda_q1", "lambda_k1", "lambda_q2", "lambda_k2")):
                    sp.dma_start(lamv[:, n, :], a[name][0, :].partition_broadcast(P)).then_inc(sem("lam_in"), 16)
                for s in range(2):
                    sp.dma_start(xr[:, s, :], x_rows[s * P:(s + 1) * P, :]).then_inc(sem(f"x_in{s}"), 16)
                for g in range(4):
                    sp.dma_start(w[:, :, g * DA:(g + 1) * DA], w_v[:, :, g * DA:(g + 1) * DA])\
                        .then_inc(sem(f"w_in{g}"), 16)
                with sp.Fori(0, NT // 2 - 1) as i:
                    for s in range(2):
                        sp.wait_ge(sem("p_xTps"), 2 * i + s + 1)
                        sp.dma_start(xr[:, s, :], x_rows[bass.ds(i * 2 * P + (2 + s) * P, P), :])\
                          .then_inc(sem(f"x_in{s}"), 16)
                sp.wait_ge(sem("p_xTps"), NT - 1)
                sp.dma_start(xr[:, 0, :], x_rows[NT * P:(NT + 1) * P, :]).then_inc(sem("x_in0"), 16)

            @block.gpsimd
            def _(pool):
                pool.memset(ident[:, :], 0.0).then_inc(sem("id0"), 1)
                pool.memset(zero[:, :], 0.0)
                pool.wait_ge(sem("id0"), 1)
                pool.affine_select(out=ident[:, :], in_=ident[:, :], compare_op=ALU.not_equal, fill=1.0,
                                   base=0, pattern=[[-1, P]], channel_multiplier=1).then_inc(sem("ident"), 1)

            @block.tensor
            def _(pe):
                pe.wait_ge(sem("ident"), 1)

                def tile(i, s):
                    t = 2 * i + s
                    pe.wait_ge(sem(f"x_in{s}"), 16 * i + 16)
                    for k in range(KC):
                        last = pe.transpose(bank[4 + k // 4][:, (k % 4) * P:(k % 4 + 1) * P],
                                            xr[:, s, k * P:(k + 1) * P], ident[:, :])
                    last.then_inc(sem("p_xTps"), 1)
                    pe.wait_ge(sem("p_xT"), t + 1)
                    for g in range(4):
                        pe.wait_ge(sem(f"w_in{g}"), 16)
                        for k in range(KC):
                            last = pe.matmul(bank[g][:, :], xT[:, k, :], w[:, k, g * DA:(g + 1) * DA],
                                             start=k == 0, stop=k == KC - 1)
                        last.then_inc(sem("p_z"), 1)
                    for g, row, b in ((0, qrow, 6), (1, krow, 7), (3, urow, 4)):
                        pe.wait_ge(sem(("p_qrow", "p_krow", None, "p_urow")[g]), t + 1)
                        for h in range(4):
                            last = pe.transpose(bank[b][:, h * P:(h + 1) * P], row[:, h * P:(h + 1) * P], ident[:, :])
                        last.then_inc(sem("p_T"), 1)
                    pe.wait_ge(sem("p_Tcopied"), 3 * t + 3)
                    pe.wait_ge(sem("p_vrow"), t + 1)

                with pe.Fori(0, NT // 2) as i:
                    tile(i, 0)
                    tile(i, 1)
                tile(NT // 2, 0)

            @block.vector
            def _(dve):
                step = Steps(dve, sem("dve_step"))
                dve.wait_ge(sem("lam_in"), 64)
                for n in range(2):
                    step(dve.tensor_tensor_reduce(out=lamw[:, :], in0=lamv[:, 2 * n, :], in1=lamv[:, 2 * n + 1, :],
                                                  scale=1.0, scalar=0.0, op0=ALU.mult, op1=ALU.add,
                                                  accum_out=lams[:, n:n + 1]))
                dve.sem_inc(sem("lam_dots"), 1)
                dve.wait_ge(sem("lam_exp"), 1)
                step(dve.tensor_tensor(lams[:, 0:1], lams[:, 3:4], lams[:, 2:3], ALU.subtract))
                step(dve.tensor_scalar(neglam[:, :], lams[:, 0:1], -LAM_INIT, None, ALU.add))

                def tile(t, tk):
                    dve.wait_ge(sem("p_xTps"), t + 1)
                    for b in range(2):
                        last = dve.tensor_copy(xT[:, 4 * b:4 * b + 4, :].rearrange("p k t -> p (k t)"), bank[4 + b][:, :])
                    last.then_inc(sem("p_xT"), 1)
                    dve.wait_ge(sem("p_z"), 4 * t + 1)
                    for h in range(H):
                        last = dve.tensor_scalar(qrow[:, h * P:(h + 1) * P], bank[0][:, h * P:(h + 1) * P],
                                                 QSCALE[h], None, ALU.mult)
                    last.then_inc(sem("p_qrow"), 1)
                    dve.wait_ge(sem("p_z"), 4 * t + 4)
                    dve.tensor_copy(urow[:, :], bank[3][:, :]).then_inc(sem("p_urow"), 1)
                    dve.wait_ge(sem("p_T"), 3 * t + 1)
                    dve.wait_ge(sem("q_out"), 16 * t + 16)
                    dve.tensor_copy(qTs[:, :, :].rearrange("p h t -> p (h t)"), bank[6][:, :])\
                       .then_inc(sem("p_Tcopied"), 1)
                    dve.sem_inc(sem("p_qTs"), 1)
                    dve.wait_ge(sem("p_T"), 3 * t + 2)
                    dve.tensor_copy(kT[:, :, bass.ds(tk * P, P)], bank[7][:, :].rearrange("p (h t) -> p h t", h=H))\
                       .then_inc(sem("p_Tcopied"), 1)
                    dve.wait_ge(sem("p_T"), 3 * t + 3)
                    for q in range(4):
                        last = dve.tensor_copy(uT[:, q, :, bass.ds(tk * (P // L), P // L)],
                                               bank[4][:, q * P:(q + 1) * P].rearrange("p (n j) -> p j n", j=L))
                    last.then_inc(sem("p_Tcopied"), 1)

                dve.sem_inc(sem("q_out"), 16)
                with dve.Fori(0, NT + 1) as t:
                    tile(t, t)

            @block.scalar
            def _(act):
                act.wait_ge(sem("lam_dots"), 1)
                act.activation(lams[:, 2:4], lams[:, 0:2], ACT.Exp).then_inc(sem("lam_exp"), 1)

                def tile(t, rows, kdst, vdst):
                    act.wait_ge(sem("p_z"), 4 * t + 2)
                    act.wait_ge(sem("k_out"), 16 * t + 16)
                    act.activation(krow[:, :], bank[1][:, :], ACT.Copy).then_inc(sem("p_krow"), 1)
                    act.wait_ge(sem("p_z"), 4 * t + 3)
                    act.activation(vrows[:, bass.ds(t, 1), :].rearrange("p o n -> p (o n)"), bank[2][:, :], ACT.Copy)\
                       .then_inc(sem("p_vrow"), 1)
                    act.wait_ge(sem("p_krow"), t + 1)
                    act.dma_start(kdst, krow[:rows, :]).then_inc(sem("k_out"), 16)
                    act.wait_ge(sem("p_vrow"), t + 1)
                    act.dma_start(vdst, vrows[:rows, bass.ds(t, 1), :].rearrange("p o n -> p (o n)"))\
                       .then_inc(sem("v_out"), 16)
                    act.wait_ge(sem("p_Tcopied"), 3 * t + 1)
                    act.wait_ge(sem("p_qTs"), t + 1)
                    act.dma_start(scr_q[:, :, bass.ds(t * P, P)], qTs[:, :, :]).then_inc(sem("q_out"), 16)

                act.sem_inc(sem("k_out"), 16)
                with act.Fori(0, NT) as t:
                    tile(t, P, k_rows[bass.ds(t * P, P), :], v_rows[bass.ds(t * P, P), :])
                tile(NT, SR, ks_rows, vs_rows)
                act.wait_ge(sem("p_Tcopied"), 3 * (NT + 1))
                for q in range(4):
                    act.dma_start(scr_u[8 * q:8 * q + 8, :, :, :].rearrange("g c j n -> (g c) j n"),
                                  uT[:, q, :, 0:NC]).then_inc(sem("u_out"), 16)
                act.wait_ge(sem("k_out"), 16 * (NT + 2))
                act.wait_ge(sem("v_out"), 16 * (NT + 1))
                act.wait_ge(sem("q_out"), 16 * (NT + 2))
                act.wait_ge(sem("u_out"), 64)


def state_space(nc, a, o, alloc, sem, ident, bank, scr_u, scr_y, scr_s):
    with ExitStack() as ctx:
        sb = alloc(ctx)
        U = sb("U", [P, G, NC])
        prow = sb("prow", [GP, 4, P])
        dtg = sb("dtg", [GP, 2])
        pcol = sb("pcol", [P, 4, GP])
        hrow = sb("hrow", [P, 2, P])
        crow = sb("crow", [P, 2, 2, 2, SP_])
        B = sb("B", [P, 2, GP, C])
        BB = sb("BB", [P, 2, GP, C])
        Cc = sb("Cc", [P, 2, GP, C])
        h0 = sb("h0", [P, 2, DB, GP])
        s1 = sb("s1", [P, 24, GP])
        pw = sb("pw", [P, 2, L + 1, GP])
        CP = sb("CP", [P, 2, GP, L + 1, C])
        BP = sb("BP", [P, 2, GP, L, C])
        W = sb("W", [P, GP, 2, 192])
        T = sb("T", [P, G, P])
        dcol = sb("dcol", [C, G])
        EX = sb("EX", [P, 2, GP, NCH])
        K0 = EX[0:C, :, :, :].rearrange("c n i k -> c (n i k)").rearrange("c (g m d) -> c g m d", g=G, m=L)
        V = sb("V", [P, 2, GP, NC])
        R8 = sb("R8", [P, GP, NCH])
        HP = W[:, :, :, :].rearrange("p i n c -> p (i n c)")[:, 0:2 * GP * NC]\
            .rearrange("p (n i c) -> p n i c", n=2, i=GP)
        tA = sb("tA", [P, GP * NCH])
        tB = sb("tB", [P, GP * NCH])
        hout = sb("hout", [P, 4, P])

        with nc.Block() as block:
            @block.sync
            def _(sp):
                for n, name in enumerate(("ssm_lambda_re", "ssm_lambda_im")):
                    sp.dma_start(prow[:, n, :], a[name][0].rearrange("(i g) p -> i (g p)", g=2)).then_inc(sem("ss_in"), 16)
                sp.dma_start(dtg[:, :], a["ssm_log_dt"][0].rearrange("(i g) -> i g", g=2)).then_inc(sem("ss_in"), 16)
                for n, name in enumerate(("ssm_b_re", "ssm_b_im")):
                    sp.dma_start(B[:, n, :, :], a[name][0].rearrange("(i g) p c -> (g p) i c", g=2)).then_inc(sem("ss_in"), 16)
                for n, name in enumerate(("ssm_c_re", "ssm_c_im")):
                    for e in range(2):
                        for i in range(8):
                            sp.dma_start(crow[C * i:C * i + C, n, e, :, :],
                                         a[name][0, 16 * e + 2 * i:16 * e + 2 * i + 2, :, :].rearrange("g c p -> c g p"))\
                              .then_inc(sem("ss_in"), 16)
                for n, name in enumerate(("state_ssm_re", "state_ssm_im")):
                    sp.dma_start(hrow[:, n, :], a[name][0].rearrange("b (i g) p -> (b i) (g p)", g=2)).then_inc(sem("ss_in"), 16)
                with nc.allow_non_contiguous_dma(reason="2 KB in all"):
                    sp.dma_start(dcol[:, :], a["ssm_d"][0].rearrange("g c -> c g")).then_inc(sem("ss_in"), 16)
                for j in range(L):
                    sp.dma_start(U[C * j:C * j + C, :, :], scr_u[:, :, j, :].rearrange("g c n -> c g n"))\
                      .then_inc(sem("U_in"), 16)
                sp.wait_ge(sem("ss_K0"), 1)
                for j in range(L):
                    sp.dma_start(T[C * j:C * j + C, :, C * j:P],
                                 K0[:, :, 0:L - j, :].rearrange("c g m d -> c g (m d)")).then_inc(sem("T_in"), 16)
                sp.wait_ge(sem("T_in"), 16 * L)
                sp.wait_ge(sem("ss_y"), GP // 3 + 1)
                for j in range(L):
                    sp.dma_start(scr_y[:, :, j, :].rearrange("g c n -> c g n"), U[C * j:C * j + C, :, :])\
                      .then_inc(sem("y_out"), 16)
                sp.wait_ge(sem("y_out"), 16 * L)
                sp.wait_ge(sem("ss_hout"), 1)
                for n in range(2):
                    sp.dma_start(o[4 + n].rearrange("d b (i g) p -> (d b i) (g p)", g=2), hout[0:GP, n, :])\
                      .then_inc(sem("h_out"), 16)
                    sp.dma_start(o[8 + n].rearrange("d b (i g) p -> (d b i) (g p)", g=2), hout[:, 2 + n, :])\
                      .then_inc(sem("h_out"), 16)
                sp.wait_ge(sem("h_out"), 64)

            @block.gpsimd
            def _(pool):
                pool.memset(T[:, :, :], 0.0).then_inc(sem("T_zero"), 1)
                pool.memset(W[:, :, :, 64:128], 0.0).then_inc(sem("W_zero"), 1)

            @block.tensor
            def _(pe):
                pe.wait_ge(sem("ss_prow"), 1)
                for n in range(3):
                    last = pe.transpose(bank[0][:, n * GP:(n + 1) * GP], prow[:, n, :], ident[:GP, :GP])
                for n in range(2):
                    last = pe.transpose(bank[1][:, n * P:(n + 1) * P], hrow[:, n, :], ident[:, :])
                for n in range(2):
                    for e in range(2):
                        last = pe.transpose(bank[2][:, (2 * n + e) * P:(2 * n + e + 1) * P],
                                            crow[:, n, e, :, :].rearrange("p g s -> p (g s)"), ident[:, :])
                last.then_inc(sem("ss_cols"), 1)
                pe.wait_ge(sem("ss_BP"), 1)
                for r in range(8):
                    if r >= 2:
                        pe.wait_ge(sem("ss_Wcopied"), r - 1)
                    for q in range(4):
                        n, i = divmod(4 * r + q, GP)
                        last = pe.transpose(bank[r % 2][:, q * P:(q + 1) * P],
                                            BP[:, n, i, :, :].rearrange("p j c -> p (j c)"), ident[:, :])
                    last.then_inc(sem("ss_Wps"), 1)
                pe.wait_ge(sem("ss_CP"), 1)
                for r in range(4):
                    if r >= 2:
                        pe.wait_ge(sem("ss_Kcopied"), r - 1)
                    for g in range(8 * r, 8 * r + 8):
                        i, s = g // 2, g % 2 * 64
                        for n in range(2):
                            last = pe.matmul(bank[2 + 4 * (r % 2) + g % 2][0:C, i % 4 * P:(i % 4 + 1) * P],
                                             BB[s:s + 64, n, i, :],
                                             CP[s:s + 64, n, i, 0:L, :].rearrange("p m c -> p (m c)"),
                                             start=n == 0, stop=n == 1)
                    last.then_inc(sem("ss_Kps"), 1)
                pe.wait_ge(sem("ss_Wcopied"), 8)
                pe.wait_ge(sem("U_in"), 16 * L)
                for i in range(GP):
                    if i >= 2:
                        pe.wait_ge(sem("ss_Vcopied"), i - 1)
                    for n in range(2):
                        for s in range(2):
                            last = pe.matmul(bank[4 + i % 2][:, n * NC:(n + 1) * NC], W[:, i, n, 64 * s:64 * s + P],
                                             U[:, 2 * i + s, :], start=s == 0, stop=s == 1)
                    last.then_inc(sem("ss_Vps"), 1)
                pe.wait_ge(sem("T_in"), 16 * L)
                pe.wait_ge(sem("ss_HP"), 1)
                for g in range(G):
                    i, s = g // 2, g % 2 * 64
                    r, q = divmod(i, 3)
                    if q == 0 and s == 0:
                        pe.wait_ge(sem("ss_Kcopied"), 4)
                        if r >= 2:
                            pe.wait_ge(sem("ss_y"), r - 1)
                    out = bank[(2, 6)[r % 2] + g % 2][:, q * NC:(q + 1) * NC]
                    pe.matmul(out, T[:, g, :], U[:, g, :], start=True, stop=False)
                    for n in range(2):
                        last = pe.matmul(out, CP[s:s + 64, n, i, 1:L + 1, :].rearrange("p m c -> p (m c)"),
                                         HP[s:s + 64, n, i, :], start=False, stop=n == 1)
                    if s and (q == 2 or g == G - 1):
                        last.then_inc(sem("ss_yps"), 1)
                pe.wait_ge(sem("ss_hs"), 1)
                for n in range(2):
                    pe.transpose(bank[0][0:GP, n * P:(n + 1) * P], s1[:, 20 + n, :], ident[:, :])
                for n in range(2):
                    last = pe.transpose(bank[1][:, n * P:(n + 1) * P],
                                        tA[:, n * P:(n + 1) * P], ident[:, :])
                last.then_inc(sem("ss_hps"), 1)

            @block.scalar
            def _(act):
                act.wait_ge(sem("ss_arg"), 1)
                act.activation(s1[:, 3, :], s1[:, 2, :], ACT.Exp).then_inc(sem("ss_dt"), 1)
                act.wait_ge(sem("ss_arg"), 2)
                act.activation(s1[:, 5, :], s1[:, 4, :], ACT.Exp).then_inc(sem("ss_mag"), 1)
                act.wait_ge(sem("ss_arg"), 3)
                act.activation(s1[:, 8, :], s1[:, 7, :], ACT.Sin)
                act.activation(s1[:, 9, :], s1[:, 7, :], ACT.Sin, scale=0.5).then_inc(sem("ss_sin"), 1)
                for r in range(8):
                    act.wait_ge(sem("ss_Wps"), r + 1)
                    if r == 0:
                        act.wait_ge(sem("W_zero"), 1)
                    n, i = divmod(4 * r, GP)
                    for s in range(2):
                        last = act.activation(W[:, i:i + 4, n, 128 * s:128 * s + 64],
                                              bank[r % 2][:, :].rearrange("p (q s c) -> p q s c", q=4, s=2)[:, :, s, :],
                                              ACT.Copy)
                    last.then_inc(sem("ss_Wcopied"), 1)
                for i in range(GP):
                    act.wait_ge(sem("ss_Vps"), i + 1)
                    act.activation(V[:, :, i, :], bank[4 + i % 2][:, 0:2 * NC].rearrange("p (n c) -> p n c", n=2),
                                   ACT.Copy).then_inc(sem("ss_Vcopied"), 1)
                for r in range(GP // 3 + 1):
                    act.wait_ge(sem("ss_yps"), r + 1)
                    n = min(3, GP - 3 * r)
                    for q in range(2):
                        last = act.activation(U[:, 6 * r:6 * r + 2 * n, :].rearrange("p (i s) c -> p i s c", s=2)[:, :, q, :],
                                              bank[(2, 6)[r % 2] + q][:, 0:n * NC].rearrange("p (i c) -> p i c", i=n),
                                              ACT.Gelu)
                    last.then_inc(sem("ss_y"), 1)

            @block.vector
            def _(dve):
                step = Steps(dve, sem("dve_step2"))
                tt, ts = dve.tensor_tensor, dve.tensor_scalar

                def cmul(ore, oim, ar, ai, br, bi, shape, neg_im=False):
                    n = int(np.prod(shape))
                    names = " ".join("wxyz"[:len(shape)])
                    kw = dict(zip("wxyz", shape))
                    t1 = tA[:, 0:n].rearrange(f"p ({names}) -> p {names}", **kw)
                    t2 = tB[:, 0:n].rearrange(f"p ({names}) -> p {names}", **kw)
                    tt(t1, ar, br, ALU.mult)
                    step(tt(t2, ai, bi, ALU.mult))
                    step(tt(ore, t1, t2, ALU.subtract))
                    tt(t1, ar, bi, ALU.mult)
                    step(tt(t2, ai, br, ALU.mult))
                    if neg_im:
                        step(tt(t1, t1, t2, ALU.add))
                        step(ts(oim, t1, -1.0, None, ALU.mult))
                    else:
                        step(tt(oim, t1, t2, ALU.add))

                dve.wait_ge(sem("ss_in"), 16 * (3 + 2 + 32 + 2 + 1))
                for s in range(2):
                    last = dve.tensor_copy(prow[:, 2, s * 64:s * 64 + 64], dtg[:, s:s + 1].broadcast_to((GP, 64)))
                last.then_inc(sem("ss_prow"), 1)
                dve.wait_ge(sem("ss_cols"), 1)
                dve.tensor_copy(s1[:, 0:3, :].rearrange("p n i -> p (n i)"), bank[0][:, 0:3 * GP])
                dve.tensor_copy(h0[:, :, :, :].rearrange("p n b i -> p (n b i)"), bank[1][:, 0:2 * P])
                step(dve.tensor_copy(Cc[:, :, :, :].rearrange("p n i c -> p (n i c)"), bank[2][:, :]))
                dve.sem_inc(sem("ss_arg"), 1)
                lr, li, dt = s1[:, 0, :], s1[:, 1, :], s1[:, 3, :]
                dve.wait_ge(sem("ss_dt"), 1)
                step(tt(s1[:, 4, :], lr, dt, ALU.mult))
                dve.sem_inc(sem("ss_arg"), 1)
                step(tt(s1[:, 6, :], li, dt, ALU.mult))
                step(ts(s1[:, 10, :], s1[:, 6, :], 1.0 / (2 * math.pi), MAGIC, ALU.mult, ALU.add))
                step(ts(s1[:, 10, :], s1[:, 10, :], -MAGIC, None, ALU.add))
                step(dve.scalar_tensor_tensor(out=s1[:, 6, :], in0=s1[:, 10, :], scalar=-PI2A, in1=s1[:, 6, :],
                                              op0=ALU.mult, op1=ALU.add))
                step(dve.scalar_tensor_tensor(out=s1[:, 6, :], in0=s1[:, 10, :], scalar=-PI2B, in1=s1[:, 6, :],
                                              op0=ALU.mult, op1=ALU.add))
                step(dve.scalar_tensor_tensor(out=s1[:, 6, :], in0=s1[:, 10, :], scalar=-PI2C, in1=s1[:, 6, :],
                                              op0=ALU.mult, op1=ALU.add))
                step(ts(s1[:, 7, :], s1[:, 6, :], 3.1415925, -3.1415925, ALU.min, ALU.max))
                dve.sem_inc(sem("ss_arg"), 1)
                dve.wait_ge(sem("ss_mag"), 1)
                dve.wait_ge(sem("ss_sin"), 1)
                sin, mag = s1[:, 8, :], s1[:, 5, :]
                cos = s1[:, 9, :]
                step(tt(s1[:, 9, :], s1[:, 9, :], s1[:, 9, :], ALU.mult))
                step(ts(cos, s1[:, 9, :], -2.0, 1.0, ALU.mult, ALU.add))
                dve.memset(pw[:, 0, 0, :], 1.0)
                dve.memset(pw[:, 1, 0, :], 0.0)
                tt(pw[:, 0, 1, :], mag, cos, ALU.mult)
                step(tt(pw[:, 1, 1, :], mag, sin, ALU.mult))
                n = 1
                while n < L:
                    w_ = [pw[:, q, n:n + 1, :].broadcast_to((P, n, GP)) for q in range(2)]
                    cmul(pw[:, 0, n + 1:2 * n + 1, :], pw[:, 1, n + 1:2 * n + 1, :],
                         pw[:, 0, 1:n + 1, :], pw[:, 1, 1:n + 1, :], w_[0], w_[1], (n, GP))
                    n *= 2
                are, aim = pw[:, 0, 1, :], pw[:, 1, 1, :]
                nre, den, t3, t4 = s1[:, 11, :], s1[:, 12, :], s1[:, 13, :], s1[:, 14, :]
                gre, gim = s1[:, 15, :], s1[:, 16, :]
                ts(nre, are, -1.0, None, ALU.add)
                tt(t3, lr, lr, ALU.mult)
                step(tt(t4, li, li, ALU.mult))
                step(tt(den, t3, t4, ALU.add))
                step(dve.reciprocal(den, den))
                tt(t3, nre, lr, ALU.mult)
                step(tt(t4, aim, li, ALU.mult))
                step(tt(gre, t3, t4, ALU.add))
                step(tt(gre, gre, den, ALU.mult))
                tt(t3, aim, lr, ALU.mult)
                step(tt(t4, nre, li, ALU.mult))
                step(tt(gim, t3, t4, ALU.subtract))
                step(tt(gim, gim, den, ALU.mult))
                gb = [g_.rearrange("p (i o) -> p i o", o=1).broadcast_to((P, GP, C)) for g_ in (gre, gim)]
                cmul(BB[:, 0, :, :], BB[:, 1, :, :], gb[0], gb[1], B[:, 0, :, :], B[:, 1, :, :], (GP, C))
                for j in range(L):
                    pj = [pw[:, q, L - 1 - j, :].rearrange("p (i o) -> p i o", o=1).broadcast_to((P, GP, C)) for q in range(2)]
                    cmul(BP[:, 0, :, j, :], BP[:, 1, :, j, :], BB[:, 0, :, :], BB[:, 1, :, :], pj[0], pj[1], (GP, C))
                dve.sem_inc(sem("ss_BP"), 1)
                for m in range(L + 1):
                    pj = [pw[:, q, m, :].rearrange("p (i o) -> p i o", o=1).broadcast_to((P, GP, C)) for q in range(2)]
                    cmul(CP[:, 0, :, m, :], CP[:, 1, :, m, :], Cc[:, 0, :, :], Cc[:, 1, :, :], pj[0], pj[1], (GP, C),
                         neg_im=True)
                dve.sem_inc(sem("ss_CP"), 1)
                for r in range(4):
                    dve.wait_ge(sem("ss_Kps"), r + 1)
                    for q in range(2):
                        last = dve.tensor_copy(
                            K0[:, 8 * r:8 * r + 8, :, :].rearrange("p (i s) m c -> p i s (m c)", s=2)[:, :, q, :],
                            bank[2 + 4 * (r % 2) + q][0:C, :].rearrange("p (i x) -> p i x", i=4))
                    last.then_inc(sem("ss_Kcopied"), 1)
                dve.wait_ge(sem("ss_Kcopied"), 4)
                skip = tA[0:C, 0:G * C].rearrange("p (g c) -> p g c", c=C)
                step(tt(skip, dcol[:, :].rearrange("p (g o) -> p g o", o=1).broadcast_to((C, G, C)),
                        ident[0:C, 0:C].rearrange("p (o c) -> p o c", o=1).broadcast_to((C, G, C)), ALU.mult))
                step(tt(K0[:, :, 0, :], K0[:, :, 0, :], skip, ALU.add))
                dve.wait_ge(sem("T_zero"), 1)
                dve.sem_inc(sem("ss_K0"), 1)
                ur = [s1[:, 17, :], s1[:, 18, :]]
                r8 = s1[:, 19, :]
                dve.tensor_copy(ur[0], cos)
                dve.tensor_copy(r8, mag)
                step(dve.tensor_copy(ur[1], sin))
                for _ in range(3):
                    step(tt(r8, r8, r8, ALU.mult))
                    cmul(t3, t4, ur[0], ur[1], ur[0], ur[1], (GP,))
                    dve.tensor_copy(ur[0], t3)
                    step(dve.tensor_copy(ur[1], t4))
                dve.wait_ge(sem("T_in"), 16 * L)
                dve.memset(EX[:, 0, :, 0:1], 1.0)
                step(dve.memset(EX[:, 1, :, 0:1], 0.0))
                n = 1
                while n < NCH:
                    w_ = [u_.rearrange("p (i o) -> p i o", o=1).broadcast_to((P, GP, n)) for u_ in ur]
                    cmul(EX[:, 0, :, n:2 * n], EX[:, 1, :, n:2 * n], EX[:, 0, :, 0:n], EX[:, 1, :, 0:n],
                         w_[0], w_[1], (GP, n))
                    if 2 * n < NCH:
                        cmul(t3, t4, ur[0], ur[1], ur[0], ur[1], (GP,))
                        dve.tensor_copy(ur[0], t3)
                        step(dve.tensor_copy(ur[1], t4))
                    n *= 2
                step(dve.tensor_copy(R8[:, :, :], r8.rearrange("p (i o) -> p i o", o=1).broadcast_to((P, GP, NCH))))
                step(dve.memset(R8[:, :, 0:1], 0.0))
                dve.wait_ge(sem("ss_Vcopied"), GP)
                vr, vi = V[:, 0, :, 0:NCH], V[:, 1, :, 0:NCH]
                er, ei = EX[:, 0, :, :], EX[:, 1, :, :]
                t1 = tA[:, 0:GP * NCH].rearrange("p (i n) -> p i n", i=GP)
                t2 = tB[:, 0:GP * NCH].rearrange("p (i n) -> p i n", i=GP)
                zr = BP[:, 0, :, :, :].rearrange("p i j c -> p i (j c)")
                zi = BP[:, 1, :, :, :].rearrange("p i j c -> p i (j c)")
                tt(t1, vr, er, ALU.mult)
                step(tt(t2, vi, ei, ALU.mult))
                step(tt(zr, t1, t2, ALU.add))
                tt(t1, vi, er, ALU.mult)
                step(tt(t2, vr, ei, ALU.mult))
                step(tt(zi, t1, t2, ALU.subtract))
                for q, z in ((0, tA), (1, tB)):
                    step(dve.tensor_tensor_scan(z[:, 0:GP * NCH], R8[:, :, :].rearrange("p i n -> p (i n)"),
                                                BP[:, q, :, :, :].rearrange("p i j c -> p (i j c)"),
                                                0.0, ALU.mult, ALU.add))
                tt(zr, t1, er, ALU.mult)
                step(tt(zi, t2, ei, ALU.mult))
                step(tt(vr, zr, zi, ALU.subtract))
                tt(zr, t1, ei, ALU.mult)
                step(tt(zi, t2, er, ALU.mult))
                step(tt(vi, zr, zi, ALU.add))
                for q in range(2):
                    dve.memset(HP[:, q, :, 0:1], 0.0)
                    dve.tensor_copy(HP[:, q, :, 1:NCH], V[:, q, :, 0:NCH - 1])
                    last = dve.tensor_copy(HP[:, q, :, NCH:NC], h0[:, q, :, :].rearrange("p b i -> p i b"))
                    dve.tensor_copy(s1[:, 20 + q, :], V[:, q, :, NCH - 1])
                step(last)
                dve.sem_inc(sem("ss_HP"), 1)
                p8 = [pw[:, q, L, :].rearrange("p (o i) -> p o i", o=1).broadcast_to((P, DB, GP)) for q in range(2)]
                h0r, h0i = h0[:, 0, :, :], h0[:, 1, :, :]
                u1 = B[:, 0, :, :].rearrange("p i c -> p (i c)")[:, 0:P].rearrange("p (b i) -> p b i", b=DB)
                u2 = B[:, 1, :, :].rearrange("p i c -> p (i c)")[:, 0:P].rearrange("p (b i) -> p b i", b=DB)
                for q, (x0, x1, op) in enumerate(((h0r, h0i, ALU.subtract), (h0i, h0r, ALU.add))):
                    tt(u1, x0, p8[0], ALU.mult)
                    step(tt(u2, x1, p8[1], ALU.mult))
                    step(tt(u1, u1, u2, op))
                    step(tt(tA[:, q * P:(q + 1) * P].rearrange("p (b i) -> p b i", b=DB), u1,
                            V[:, q, :, NCH:NC].rearrange("p i b -> p b i"), ALU.add))
                dve.sem_inc(sem("ss_hs"), 1)
                dve.wait_ge(sem("ss_hps"), 1)
                dve.tensor_copy(hout[0:GP, 0:2, :].rearrange("p n s -> p (n s)"), bank[0][0:GP, 0:2 * P])
                dve.tensor_copy(hout[:, 2:4, :].rearrange("p n s -> p (n s)"), bank[1][:, 0:2 * P])\
                   .then_inc(sem("ss_hout"), 1)

    with ExitStack() as ctx:
        sb = alloc(ctx)
        yT = sb("yT", [P, 4, L * NC])
        wg = sb("wg", [P, 4, DA])
        bg = sb("bg", [P, 4])
        gate = sb("gate", [P, 2, 4, 272])
        sT = sb("sT", [P, 4, TP])
        NQ = L * NC // 4
        with nc.Block() as block:
            @block.sync
            def _(sp):
                for q in range(4):
                    sp.dma_start(yT[:, q, :], scr_y[8 * q:8 * q + 8, :, :, :].rearrange("g c j n -> (g c) (j n)"))\
                      .then_inc(sem("yT_in"), 16)
                sp.dma_start(wg[:, :, :], a["ssm_w_glu"].rearrange("o (k p) n -> p (o k) n", p=P)).then_inc(sem("yT_in"), 16)
                with nc.allow_non_contiguous_dma(reason="2 KB in all"):
                    sp.dma_start(bg[:, :], a["ssm_b_glu"][0].rearrange("(q p) -> p q", p=P)).then_inc(sem("yT_in"), 16)
                sp.wait_ge(sem("gl_s"), 5)
                sp.dma_start(scr_s, sT[:, :, :]).then_inc(sem("s_out"), 16)
                sp.wait_ge(sem("s_out"), 16)

            @block.tensor
            def _(pe):
                pe.wait_ge(sem("yT_in"), 96)
                for b in range(4):
                    for q in range(4):
                        n = 4 * b + q
                        if n >= 8:
                            pe.wait_ge(sem("gl_gate"), n - 7)
                        for k in range(4):
                            last = pe.matmul(bank[n % 8][:, 0:NQ], wg[:, k, q * P:(q + 1) * P],
                                             yT[:, k, b * NQ:(b + 1) * NQ], start=k == 0, stop=k == 3)
                        last.then_inc(sem("gl_ps"), 1)

            @block.scalar
            def _(act):
                for b in range(4):
                    if b >= 2:
                        act.wait_ge(sem("gl_s"), b)
                    for q in range(4):
                        n = 4 * b + q
                        act.wait_ge(sem("gl_ps"), n + 1)
                        act.activation(gate[:, b % 2, q, :], bank[n % 8][:, 0:NQ], ACT.Sigmoid, bias=bg[:, q:q + 1])\
                           .then_inc(sem("gl_gate"), 1)

            @block.vector
            def _(dve):
                dve.memset(sT[:, :, SEQ + SR:TP], 0.0).then_inc(sem("gl_s"), 1)
                for b in range(4):
                    dve.wait_ge(sem("gl_gate"), 4 * b + 4)
                    for q in range(4):
                        last = dve.tensor_tensor(
                            sT[:, q, 0:SEQ + SR].rearrange("p (n j) -> p j n", j=L)[:, 2 * b:2 * b + 2, :],
                            yT[:, q, b * NQ:(b + 1) * NQ].rearrange("p (j n) -> p j n", j=2),
                            gate[:, b % 2, q, :].rearrange("p (j n) -> p j n", j=2), ALU.mult)
                    last.then_inc(sem("gl_s"), 1)


def trunk(nc, a, o, alloc, sem, ident, kT, vrows, neglam, bank, psum, scr_q, scr_s):
    with ExitStack() as ctx:
        sb = alloc(ctx)
        w_out = sb("w_out_sb", [P, KC, DM])
        keysT = sb("keysT", [P, 2 * EH, NKEY])
        wq = sb("wq", [P, 2, KC, 2 * NKEY])
        lng = sb("lng", [P, 4, DM])
        subg = sb("subg", [P, DV])
        gk = sb("gk", [P, 2])
        dist = sb("dist", [P, SEQ])
        bias = sb("bias", [P, SEQ + DS])
        xin = sb("xin", [P, DM])
        qT = sb("qT", [P, H, P])
        sT = sb("sT_t", [P, 4, P])
        oT = sb("oT", [P, 4, P])
        E = sb("E", [P, 2 * SEQ])
        aT = sb("aT", [P, KC, P])
        x1 = sb("x1", [P, DM])
        x1c = sb("x1c", [P, DM])
        junk = sb("junk", [P, 2, DM], mybir.dt.bfloat16)
        y = sb("y", [P, DM])
        Ur = sb("Ur", [P, RING, DM])
        Vr = sb("Vr", [P, RING, DM])
        D = sb("D", [P, RING, P])
        small = sb("small", [P, 64])
        bn = sb("bn", [P, 2, 6])
        mv = sb("mv", [P, 2])
        bn2 = sb("bn2", [P, 2, 6])
        mv2 = sb("mv2", [P, 2])
        qh = sb("qh", [P, 2 * NKEY])
        qTh = sb("qTh", [P, 2, P])
        sc = sb("sc", [P, 2, 2 * NKEY])
        sc2 = sb("sc2", [P, 2 * NKEY])
        cand = sb("cand", [P, TOP * TOP])
        vt = sb("vt", [P, 2 * EH, TOP])
        it = sb("it", [P, 2 * EH, TOP], U32)
        itf = sb("itf", [P, 2 * EH, TOP])
        best = sb("best", [P, EH, TOP])
        pos = sb("pos", [P, EH, TOP], U32)
        pint = sb("pint", [P, NK], U32)
        pf = sb("pf", [P, NK])
        key = sb("key", [P, 2, NK])
        gates = sb("gates", [P, EH, TOP])
        gcur = sb("gcur", [P, NK])
        icur = sb("icur", [P, NK], U32)
        iot_i = sb("iot_i", [P, TOP], I32)
        iot = sb("iot", [P, TOP])
        idx = sb("idx", [P, 2, GR], U32)
        acts = sb("acts", [P, GR])
        ge = sb("ge", [P, GR])
        qbd = sb("qbd", [P, H, 64])
        vnew = sb("vnew", [DS, DA])
        PTn = sb("PTn", [DS, 64])
        sel = sb("sel", [64, P])
        rowc = sb("rowc", [64, 8])
        headm = sb("headm", [64, H])
        wm = sb("wm", [64, H])
        rowi = sb("rowi", [64, 2], I32)
        coli = dist[0:64, :].bitcast(I32)
        pidx = sb("pidx", [P, DB * PG], U32)
        Kst = wq[:, :, :, :].rearrange("p s k n -> p s (k n)").rearrange("p s (g n) -> p s g n", n=DA)

        Ef = E[:, :]

        def S2(c):
            return psum[:, 2 * c:2 * c + 2, :].rearrange("p b n -> p (b n)")

        y_prompt = o[0].rearrange("b t d -> (b t) d")
        y_sample = o[1].rearrange("b t d -> (b t) d")
        wq_v = a["peer_w_q"][0].rearrange("(k p) n -> p k n", p=P)
        ku = a["cache_k"].rearrange("d g t h c q -> (d g t) (h c q)")
        vu = a["cache_v"].rearrange("d g t h v -> (d g t) (h v)")
        U_tab = a["peer_u"][0]
        V_tab = a["peer_v"][0]

        def wait(eng, name, value, hold=False):
            if isinstance(value, int) and value <= 0:
                return
            eng.wait_ge(sem(name), value)
            if hold and not isinstance(value, int):
                eng.sem_inc(sem("held_" + str(hold)), 1)

        def sp_front(sp, t, rows):
            src = a["x_all"][bass.ds(t * P, P), :]
            if rows == P:
                wait(sp, "scores", 4 * t)
            else:
                wait(sp, "scores", 4 * NT)
            sp.dma_start(qT[:, :, :], scr_q[:, :, bass.ds(t * P, P)]).then_inc(sem("q_in"), 16)
            wait(sp, "h_ready", 2 * t)
            sp.dma_start(sT[:, :, :], scr_s[:, :, bass.ds(t * P, P)]).then_inc(sem("sT_in"), 16)
            wait(sp, "x1_ready", t)
            sp.dma_start(xin[:, :], src).then_inc(sem("xin"), 16)
            if rows != P:
                for b in range(DB):
                    wait(sp, "s_O", b)
                    sp.dma_start(vnew[:, :], vrows[DS * b:DS * b + DS, NT, :]).then_inc(sem("vnew_in"), 16)
                wait(sp, "s_KTps", 8 * DB)
            for e in range(EH):
                wait(sp, "q_ps", 8 * t + e - 1)
                sp.dma_start(wq[:, e % 2, :, :], wq_v[:, :, 2 * NKEY * e:2 * NKEY * (e + 1)])\
                  .then_inc(sem(f"wq_in{e % 2}"), 16)

        def sp_store(sp, t, rows):
            wait(sp, "y_ready", t + 1)
            dst = y_prompt[bass.ds(t * P, P), :] if rows == P else y_sample
            sp.dma_start(dst, y[:rows, :]).then_inc(sem("y_out3"), 16)

        def pool_group(pool, t, g, rows, b):
            pool.tensor_copy(idx[:, b, :], icur[:, bass.ds(GR * g, GR)]).then_inc(sem("idx_ready"), 1)
            wait(pool, "idx_ready", NK // GR * t + g + 1, hold="pool")
            for j in range(GR):
                k = NK * t + GR * g + j
                for tab, ring, free, arr in ((U_tab, Ur, "dot_done", "u_in"), (V_tab, Vr, "vsum_done", "v_in")):
                    wait(pool, free, k + 1, hold="pool")
                    pool.indirect_dma_start(out=ring[:rows, j % RING, :], out_offset=None, in_=tab,
                                            in_offset=bass.IndirectOffsetOnAxis(ap=idx[:rows, b, j:j + 1], axis=0))\
                        .then_inc(sem(f"{arr}{j % RING}"), 16)

        def pool_sample(pool, b):
            for pg in range(PG):
                if pg % 4 == 0:
                    wait(pool, "s_KTps", 8 * b - 4 + pg)
                pool.indirect_dma_start(out=Kst[:, pg // 4, pg % 4, :], out_offset=None, in_=ku,
                                        in_offset=bass.IndirectOffsetOnAxis(ap=pidx[:, PG * b + pg:PG * b + pg + 1], axis=0))\
                    .then_inc(sem(f"s_K{pg // 4}"), 16)
            wait(pool, "s_O", b)
            for pg in range(PG):
                pool.indirect_dma_start(out=vrows[:, pg, :], out_offset=None, in_=vu,
                                        in_offset=bass.IndirectOffsetOnAxis(ap=pidx[:, PG * b + pg:PG * b + pg + 1], axis=0))\
                    .then_inc(sem("s_V"), 16)

        def pe_attention(pe, t, h):
            wait(pe, "q_in", 16 * t + 16)
            if h == 0:
                wait(pe, "sc_ready", EH * t)
            wait(pe, "aT_ready", 4 * t + h, hold="pe")
            for c in range(2):
                for e in range(2):
                    last = pe.matmul(bank[2 * c + e][:, :], qT[64 * c:64 * c + 64, h, :],
                                     kT[64 * c:64 * c + 64, h, 512 * e:512 * e + 512], start=True, stop=True)
            last.then_inc(sem("scores"), 1)
            wait(pe, "map_ready", 4 * t + h + 1, hold="pe")
            for j in range(NT):
                last = pe.transpose(bank[j // 4][:, j % 4 * P:(j % 4 + 1) * P], Ef[:, SEQ + j * P:SEQ + (j + 1) * P], ident[:, :])
            last.then_inc(sem("aT_ps"), 1)
            wait(pe, "aT_ready", 4 * t + h + 1, hold="pe")
            for j in range(NT):
                last = pe.matmul(bank[4][:, h * DV:(h + 1) * DV], aT[:, j, :], vrows[:, j, h * DV:(h + 1) * DV],
                                 start=j == 0, stop=j == NT - 1)
            last.then_inc(sem("o_ready"), 1)

        def pe_sample(pe, b):
            wait(pe, "q_in", 16 * NT + 16)
            for pg in range(PG):
                if pg % 4 == 0:
                    wait(pe, f"s_K{pg // 4}", 64 * (b + 1))
                wait(pe, "s_KT", 8 * b + pg - 1)
                for h in range(H):
                    last = pe.transpose(bank[(3, 5)[pg % 2]][:, h * P:(h + 1) * P],
                                        Kst[:, pg // 4, pg % 4, h * P:(h + 1) * P], ident[:, :])
                last.then_inc(sem("s_KTps"), 1)
            wait(pe, "s_KT", 8 * b + 8)
            wait(pe, "s_qbd", b + 1)
            wait(pe, "s_Om", b)
            for e, (k0, n) in enumerate(((0, 512), (512, 512), (SEQ + DS * b, DS))):
                for h in range(H):
                    last = pe.matmul(bank[e][0:64, 0:n], qbd[:, h, :], kT[:, h, k0:k0 + n], start=h == 0, stop=h == H - 1)
            last.then_inc(sem("s_scores"), 1)
            wait(pe, "s_exp", b + 1)
            for pg in range(PG):
                pe.transpose(bank[0][:, 64 * pg:64 * pg + 64], Ef[0:64, P * pg:P * pg + P], ident[0:64, 0:64])
            pe.transpose(bank[1][0:DS, 0:64], Ef[0:64, SEQ:SEQ + DS], ident[0:64, 0:64]).then_inc(sem("s_PTps"), 1)
            wait(pe, "s_PT", b + 1)
            wait(pe, "s_V", 128 * (b + 1))
            wait(pe, "vnew_in", 16 * (b + 1))
            for pg in range(PG):
                pe.matmul(bank[2][0:64, :], aT[:, pg, 0:64], vrows[:, pg, :], start=pg == 0, stop=False)
            pe.matmul(bank[2][0:64, :], PTn[:, :], vnew[:, :], start=False, stop=True).then_inc(sem("s_O"), 1)
            wait(pe, "s_Om", b + 1)
            pe.matmul(bank[4][0:64, :], sel[:, 56 - DS * b:120 - DS * b], Ef[0:64, SEQ + 16:SEQ + 16 + DA],
                      start=b == 0, stop=b == DB - 1).then_inc(sem("s_acc"), 1)

        def pe_output(pe, t, rows):
            wait(pe, "on_ready", t + 1, hold="pe")
            for h in range(H):
                last = pe.transpose(bank[5][:, h * P:h * P + rows], Ef[:rows, h * P:(h + 1) * P], ident[:rows, :rows])
            last.then_inc(sem("oT_ps"), 1)
            wait(pe, "oT_ready", t + 1)
            wait(pe, "sT_in", 16 * t + 16, hold="pe")
            for e in range(2):
                for k in range(KC):
                    cols = (oT if k < 4 else sT)[:, k % 4, :rows]
                    last = pe.matmul(bank[e][:rows, :], cols, w_out[:, k, 512 * e:512 * e + 512],
                                     start=k == 0, stop=k == KC - 1)
                last.then_inc(sem("h_ready"), 1)
            wait(pe, "x1_ready", t + 1, hold="pe")
            for k in range(KC):
                last = pe.transpose(bank[2 + k // 4][:, k % 4 * P:k % 4 * P + rows], x1[:rows, k * P:(k + 1) * P],
                                    ident[:rows, :rows])
            last.then_inc(sem("x1T_ps"), 1)
            wait(pe, "x1T_ready", t + 1, hold="pe")

        def pe_head(pe, t, e, rows):
            n = EH * t + e
            wait(pe, f"wq_in{e % 2}", 64 * t + 16 * (e // 2) + 16)
            wait(pe, "q_copied", n, hold="pe")
            for k in range(KC):
                last = pe.matmul(bank[4][:rows, 0:2 * NKEY], aT[:, k, :rows], wq[:, e % 2, k, :], start=k == 0, stop=k == KC - 1)
            last.then_inc(sem("q_ps"), 1)
            wait(pe, "q_copied", n + 1, hold="pe")
            for c in range(2):
                last = pe.transpose(bank[5][:, c * P:c * P + rows], qh[:rows, c * NKEY:(c + 1) * NKEY], ident[:rows, :rows])
            last.then_inc(sem("qT_ps"), 1)
            wait(pe, "qT_ready", n + 1, hold="pe")
            for c in range(2):
                last = pe.matmul(bank[0][:rows, c * NKEY:(c + 1) * NKEY], qTh[:, c, :rows], keysT[:, 2 * e + c, :],
                                 start=True, stop=True)
            last.then_inc(sem("sc_ps"), 1)
            wait(pe, "sc_ready", n + 1, hold="pe")

        def pe_group(pe, t, g, rows, first=False, last=False):
            for j in range(GR):
                k = NK * t + GR * g + j
                wait(pe, f"v_in{j % RING}", 16 * (NK // RING * t + 2 * g + j // RING + 1))
                wait(pe, "diag_done", k + 1, hold="pe")
                for e in range(2):
                    ins = pe.matmul(bank[6 + e][:rows, :], D[:rows, j % RING, :rows], Vr[:rows, j % RING, 512 * e:512 * e + 512],
                                    start=first and j == 0, stop=last and j == GR - 1)
                ins.then_inc(sem("vsum_done"), 1)

        def act_attention(act, t, h):
            wait(act, "max_ready", 4 * t + h + 1)
            for c in range(2):
                last = act.activation(Ef[:, c * SEQ:(c + 1) * SEQ], Ef[:, c * SEQ:(c + 1) * SEQ], ACT.Exp,
                                      bias=small[:, 2 + c:3 + c], accum_out=small[:, 4 + c:5 + c])
            last.then_inc(sem("exp_ready"), 1)
            wait(act, "aT_ps", 4 * t + h + 1)
            for e in range(2):
                last = act.activation(aT[:, 4 * e:4 * e + 4, :].rearrange("p k t -> p (k t)"), bank[e][:, :], ACT.Copy)
            last.then_inc(sem("aT_ready"), 1)

        def act_sample(act, b):
            for pg in range(PG):
                if pg == 0:
                    wait(act, "s_scores", b)
                wait(act, "s_KTps", 8 * b + pg + 1)
                act.activation(kT[:, :, pg * P:(pg + 1) * P], bank[(3, 5)[pg % 2]][:, :].rearrange("p (h t) -> p h t", h=H),
                               ACT.Copy).then_inc(sem("s_KT"), 1)
            wait(act, "s_max", b + 1)
            act.activation(Ef[0:64, 0:SEQ + DS], Ef[0:64, 0:SEQ + DS], ACT.Exp, bias=small[0:64, 2:3],
                           accum_out=small[0:64, 4:5]).then_inc(sem("s_exp"), 1)
            wait(act, "s_PTps", b + 1)
            act.activation(aT[:, :, 0:64], bank[0][:, :].rearrange("p (g r) -> p g r", g=PG), ACT.Copy)
            act.activation(PTn[:, :], bank[1][0:DS, 0:64], ACT.Copy).then_inc(sem("s_PT"), 1)

        def act_output(act, t, rows):
            wait(act, "ss_ready", t + 1)
            act.activation(small[:rows, 12:16], small[:rows, 8:12], ACT.Sqrt).then_inc(sem("sr_ready"), 1)
            wait(act, "var_ready", t + 1)
            act.activation(small[:rows, 17:18], small[:rows, 16:17], ACT.Sqrt).then_inc(sem("sd_ready"), 1)
            wait(act, "x1T_ps", t + 1)
            for e in range(2):
                last = act.activation(aT[:, 4 * e:4 * e + 4, :rows],
                                      bank[2 + e][:, :].rearrange("p (k t) -> p k t", k=4)[:, :, :rows], ACT.Copy)
            last.then_inc(sem("x1T_ready"), 1)

        def act_head(act, t, e, rows):
            n = EH * t + e
            wait(act, "q_ps", n + 1)
            act.activation(qh[:rows, :], bank[4][:rows, 0:2 * NKEY], ACT.Square, accum_out=small[:rows, 24 + e:25 + e])\
               .then_inc(sem("q_sq"), 1)
            wait(act, "q_sq", n + 1)
            act.activation(qh[:rows, :], bank[4][:rows, 0:2 * NKEY], ACT.Copy).then_inc(sem("q_copied"), 1)
            wait(act, "qT_ps", n + 1)
            act.activation(qTh[:, :, :rows], bank[5][:, 0:2 * P].rearrange("p (c t) -> p c t", c=2)[:, :, :rows], ACT.Copy)\
               .then_inc(sem("qT_ready"), 1)
            wait(act, "sc_ps", n + 1)
            wait(act, "topk_done", n - 1)
            act.activation(sc[:rows, e % 2, :], bank[0][:rows, 0:2 * NKEY], ACT.Copy).then_inc(sem("sc_ready"), 1)

        def act_combine(act, t, rows):
            wait(act, "qs_ready", t + 1)
            act.activation(small[:rows, 40:48], small[:rows, 32:40], ACT.Sqrt).then_inc(sem("qr_ready"), 1)
            wait(act, "lg_ready", t + 1)
            act.activation(gates[:rows, :, :], best[:rows, :, :], ACT.Exp).then_inc(sem("ex_ready"), 1)

        def act_group(act, t, g, rows):
            for r in range(GR // 2):
                wait(act, "dot_done", NK * t + GR * g + 2 * r + 2 + RING)
                act.activation(ge[:rows, 2 * r:2 * r + 2], acts[:rows, 2 * r:2 * r + 2], ACT.Gelu).then_inc(sem("gelu_done"), 1)

        def act_finish(act, t, rows):
            wait(act, "var2_ready", t + 1)
            act.activation(small[:rows, 19:20], small[:rows, 18:19], ACT.Sqrt).then_inc(sem("sd2_ready"), 1)

        def dve_attention(dve, step, t, h):
            if h == 0:
                if not (isinstance(t, int) and t == 0):
                    step(dve.tensor_scalar(dist[:, :], dist[:, :], -float(P), None, ALU.add))
                step(dve.tensor_scalar(bias[:, 0:SEQ], dist[:, :], 0.0, MASKED, ALU.is_gt, ALU.mult))
                step(dve.tensor_tensor(bias[:, 0:SEQ], bias[:, 0:SEQ], dist[:, :], ALU.add))
            wait(dve, "aT_ps", 4 * t + h)
            wait(dve, "scores", 4 * t + h + 1, hold="dve")
            for c in range(2):
                ins = dve.tensor_tensor_reduce(out=Ef[:, c * SEQ:(c + 1) * SEQ], in0=S2(c), in1=bias[:, 0:SEQ],
                                               scale=SLOPE[h], scalar=LOW, op0=ALU.add, op1=ALU.max,
                                               accum_out=small[:, c:c + 1])
            step(ins)
            dve.tensor_scalar(small[:, 2:4], small[:, 0:2], -1.0, None, ALU.mult).then_inc(sem("max_ready"), 1)
            wait(dve, "exp_ready", 4 * t + h + 1)
            step(dve.reciprocal(small[:, 6:8], small[:, 4:6]))
            step(dve.tensor_scalar(small[:, 7:8], small[:, 7:8], neglam[:, 0:1], None, ALU.mult))
            step(dve.tensor_scalar(Ef[:, 0:SEQ], Ef[:, 0:SEQ], small[:, 6:7], None, ALU.mult))
            dve.scalar_tensor_tensor(out=Ef[:, SEQ:], in0=Ef[:, SEQ:], scalar=small[:, 7:8], in1=Ef[:, 0:SEQ],
                                     op0=ALU.mult, op1=ALU.add).then_inc(sem("map_ready"), 1)

        def dve_sample_setup(dve, step):
            q, slope, mw = rowc[:, 0:1], rowc[:, 1:2], rowc[:, 2:3]
            wait(dve, "aT_ps", 4 * NT)
            wait(dve, "s_iota", 1)
            step(dve.tensor_copy(bias[0:64, 0:SEQ], coli))
            step(dve.tensor_copy(bias[0:64, SEQ:], iot_i[0:64, 0:DS]))
            step(dve.tensor_scalar(bias[0:64, 0:SEQ], bias[0:64, 0:SEQ], -float(PAST), None, ALU.add))
            step(dve.tensor_scalar(bias[0:64, :], bias[0:64, :], q, None, ALU.subtract))
            step(dve.tensor_scalar(Ef[0:64, 0:SEQ + DS], bias[0:64, :], 0.0, MASKED, ALU.is_gt, ALU.mult))
            step(dve.tensor_tensor(bias[0:64, :], bias[0:64, :], Ef[0:64, 0:SEQ + DS], ALU.add))

        def dve_sample(dve, step, b):
            wait(dve, "q_in", 16 * NT + 16)
            wait(dve, "s_scores", b)
            flat = qbd[:, :, :].rearrange("p h r -> p (h r)")
            for c in range(2):
                for h in range(H):
                    last = dve.tensor_copy(flat[64 * c:64 * c + 64, 80 * h + DS * c:80 * h + DS * c + DS],
                                           qT[64 * c:64 * c + 64, h, DS * b:DS * b + DS])
            last.then_inc(sem("s_qbd"), 1)
            wait(dve, "s_acc", b)
            wait(dve, "s_scores", b + 1)
            S = psum[0:64, 0:3, :].rearrange("p b n -> p (b n)")[:, 0:SEQ + DS]
            step(dve.tensor_tensor(Ef[0:64, 0:SEQ + DS], S, bias[0:64, :], ALU.add))
            step(dve.tensor_scalar(Ef[0:64, 0:SEQ + DS], Ef[0:64, 0:SEQ + DS], rowc[:, 1:2], None, ALU.mult))
            step(dve.reduce_max(small[0:64, 0:1], Ef[0:64, 0:SEQ + DS], X))
            dve.tensor_scalar(small[0:64, 2:3], small[0:64, 0:1], -1.0, None, ALU.mult).then_inc(sem("s_max"), 1)
            wait(dve, "s_exp", b + 1)
            step(dve.reciprocal(small[0:64, 6:7], small[0:64, 4:5]))
            step(dve.tensor_scalar(small[0:64, 6:7], small[0:64, 6:7], rowc[:, 2:3], None, ALU.mult))
            step(dve.tensor_scalar(wm[:, :], headm[:, :], small[0:64, 6:7], None, ALU.mult))
            wait(dve, "s_O", b + 1)
            dve.tensor_tensor(Ef[0:64, SEQ + 16:SEQ + 16 + DA].rearrange("p (h v) -> p h v", h=H),
                              bank[2][0:64, :].rearrange("p (h v) -> p h v", h=H),
                              wm[:, :].rearrange("p (h u) -> p h u", u=1).broadcast_to((64, H, DV)), ALU.mult)\
               .then_inc(sem("s_Om"), 1)

        def layer_norm(dve, step, r, rows, gain, stats, agg, col, var_sem, sd_sem, n):
            for e in range(2):
                ins = dve.bn_stats(stats[:rows, e, :], r[:rows, 512 * e:512 * e + 512])
            step(ins)
            step(dve.bn_aggr(agg[:rows, :], stats[:rows, :, :].rearrange("p a b -> p (a b)")))
            dve.tensor_scalar(small[:rows, col:col + 1], agg[:rows, 1:2], EPS, None, ALU.add).then_inc(sem(var_sem), 1)
            wait(dve, sd_sem, n)
            step(dve.reciprocal(small[:rows, col + 1:col + 2], small[:rows, col + 1:col + 2]))
            step(dve.tensor_scalar(r[:rows, :], r[:rows, :], agg[:rows, 0:1], small[:rows, col + 1:col + 2],
                                   ALU.subtract, ALU.mult))
            step(dve.tensor_tensor(r[:rows, :], r[:rows, :], lng[:rows, gain, :], ALU.mult))
            return dve.tensor_tensor(r[:rows, :], r[:rows, :], lng[:rows, gain + 1, :], ALU.add)

        def dve_output(dve, step, t, rows):
            if rows == P:
                wait(dve, "o_ready", 4 * t + 4)
            else:
                wait(dve, "s_acc", DB)
            step(dve.tensor_copy(Ef[:rows, 0:DA], bank[4][:rows, :]))
            step(dve.tensor_tensor(Ef[:rows, DA:2 * DA], Ef[:rows, 0:DA], Ef[:rows, 0:DA], ALU.mult))
            step(dve.reduce_sum(small[:rows, 8:12], Ef[:rows, DA:2 * DA].rearrange("p (h v) -> p h v", h=H), X))
            dve.tensor_scalar(small[:rows, 8:12], small[:rows, 8:12], 1.0 / DV, EPS, ALU.mult, ALU.add)\
               .then_inc(sem("ss_ready"), 1)
            wait(dve, "sr_ready", t + 1)
            step(dve.reciprocal(small[:rows, 12:16], small[:rows, 12:16]))
            for h in range(H):
                ins = dve.scalar_tensor_tensor(out=Ef[:rows, h * DV:(h + 1) * DV], in0=Ef[:rows, h * DV:(h + 1) * DV],
                                               scalar=small[:rows, 12 + h:13 + h], in1=subg[:rows, :],
                                               op0=ALU.mult, op1=ALU.mult)
            ins.then_inc(sem("on_ready"), 1)
            wait(dve, "oT_ps", t + 1)
            dve.tensor_copy(oT[:, :, :rows], bank[5][:, :].rearrange("p (h t) -> p h t", h=H)[:, :, :rows])\
               .then_inc(sem("oT_ready"), 1)
            wait(dve, "xin", 16 * t + 16)
            wait(dve, "h_ready", 2 * t + 2)
            for e in range(2):
                ins = dve.scalar_tensor_tensor(out=x1[:rows, 512 * e:512 * e + 512], in0=xin[:rows, 512 * e:512 * e + 512],
                                               scalar=ALPHA, in1=bank[e][:rows, :], op0=ALU.mult, op1=ALU.add)
            step(ins)
            layer_norm(dve, step, x1, rows, 0, bn, mv, 16, "var_ready", "sd_ready", t + 1).then_inc(sem("x1_ready"), 1)

        def dve_topk(dve, step, src, scratch, vals, idxs):
            step(dve.max(vals[:, 0:8], src))
            step(dve.max_index(idxs[:, 0:8], vals[:, 0:8], src))
            step(dve.match_replace(scratch, vals[:, 0:8], src, LOW))
            step(dve.max(vals[:, 8:16], scratch))
            step(dve.max_index(idxs[:, 8:16], vals[:, 8:16], scratch))

        def dve_head(dve, step, t, e, rows):
            wait(dve, "sc_ready", EH * t + e + 1, hold="dve")
            for c in range(2):
                dve_topk(dve, step, sc[:rows, e % 2, c * NKEY:(c + 1) * NKEY], sc2[:rows, 0:NKEY],
                         vt[:rows, 2 * e + c, :], it[:rows, 2 * e + c, :])
            dve.sem_inc(sem("topk_done"), 1)
            cv = cand[:rows, :].rearrange("p (i j) -> p i j", i=TOP)
            step(dve.tensor_tensor(cv, vt[:rows, 2 * e, :].rearrange("p (i u) -> p i u", u=1).broadcast_to((rows, TOP, TOP)),
                                   vt[:rows, 2 * e + 1, :].rearrange("p (u j) -> p u j", u=1).broadcast_to((rows, TOP, TOP)),
                                   ALU.add))
            dve_topk(dve, step, cand[:rows, :], sc2[:rows, :], best[:rows, e, :], pos[:rows, e, :])

        def dve_combine(dve, step, t, rows):
            wait(dve, "q_copied", EH * t + EH)
            dve.tensor_scalar(small[:rows, 32:40], small[:rows, 24:32], 1.0 / (2 * NKEY), EPS, ALU.mult, ALU.add)\
               .then_inc(sem("qs_ready"), 1)
            step(dve.tensor_copy(itf[:rows, :, :], it[:rows, :, :]))
            eq = Ef[:rows, 0:NK * TOP].rearrange("p (e k i) -> p e k i", e=EH, k=TOP)
            for c, (op, n) in enumerate(((ALU.logical_shift_right, 4), (ALU.bitwise_and, 15))):
                step(dve.tensor_scalar(pint[:rows, :], pos[:rows, :, :].rearrange("p e k -> p (e k)"), n, None, op))
                step(dve.tensor_copy(pf[:rows, :], pint[:rows, :]))
                step(dve.tensor_tensor(eq, pf[:rows, :].rearrange("p (e k u) -> p e k u", e=EH, u=1).broadcast_to((rows, EH, TOP, TOP)),
                                       iot[:rows, :].rearrange("p (a b i) -> p a b i", a=1, b=1).broadcast_to((rows, EH, TOP, TOP)),
                                       ALU.is_equal))
                keys = itf[:rows, :, :].rearrange("p (e c) i -> p e c i", c=2)[:, :, c:c + 1, :].broadcast_to((rows, EH, TOP, TOP))
                step(dve.tensor_tensor(eq, eq, keys, ALU.mult))
                step(dve.reduce_sum(key[:rows, c, :], eq, X))
            step(dve.scalar_tensor_tensor(out=key[:rows, 0, :], in0=key[:rows, 0, :], scalar=float(NKEY), in1=key[:rows, 1, :],
                                          op0=ALU.mult, op1=ALU.add))
            wait(dve, "qr_ready", t + 1)
            step(dve.reciprocal(small[:rows, 40:48], small[:rows, 40:48]))
            step(dve.tensor_copy(small[:rows, 48:56], best[:rows, :, 0]))
            step(dve.tensor_tensor(best[:rows, :, :], best[:rows, :, :],
                                   small[:rows, 48:56].rearrange("p (e u) -> p e u", u=1).broadcast_to((rows, EH, TOP)), ALU.subtract))
            dve.tensor_tensor(best[:rows, :, :], best[:rows, :, :],
                              small[:rows, 40:48].rearrange("p (e u) -> p e u", u=1).broadcast_to((rows, EH, TOP)), ALU.mult)\
               .then_inc(sem("lg_ready"), 1)
            wait(dve, "ex_ready", t + 1)
            step(dve.reduce_sum(small[:rows, 48:56], gates[:rows, :, :], X))
            step(dve.reciprocal(small[:rows, 48:56], small[:rows, 48:56]))
            step(dve.tensor_tensor(gates[:rows, :, :], gates[:rows, :, :],
                                   small[:rows, 48:56].rearrange("p (e u) -> p e u", u=1).broadcast_to((rows, EH, TOP)), ALU.mult))

        def dve_begin(dve, step, t, rows):
            wait(dve, "vsum_done", NK * t + RING)
            dve.tensor_copy(x1c[:rows, :], x1[:rows, :])
            dve.tensor_copy(gcur[:rows, :], gates[:rows, :, :].rearrange("p e k -> p (e k)"))
            step(dve.tensor_copy(icur[:rows, :], key[:rows, 0, :]))
            dve.sem_inc(sem("cur_ready"), 1)

        def dve_group(dve, t, g, rows):
            def diagonals(r):
                wait(dve, "gelu_done", NK // 2 * t + GR // 2 * g + r + 1)
                for j in (2 * r, 2 * r + 1):
                    wait(dve, "vsum_done", NK * t + GR * g + j + 1)
                    dve.tensor_scalar(D[:rows, j % RING, :rows], ident[:rows, :rows], ge[:rows, j:j + 1],
                                      gcur[:rows, bass.ds(GR * g + j, 1)], ALU.mult, ALU.mult).then_inc(sem("diag_done"), 1)

            for r in range(GR // 2):
                for j in (2 * r, 2 * r + 1):
                    wait(dve, f"u_in{j % RING}", 16 * (NK // RING * t + 2 * g + j // RING + 1), hold="dve")
                    wait(dve, "dot_done", NK * t + GR * g + j + RING - 1, hold="dve")
                    dve.tensor_tensor_reduce(out=junk[:rows, j % 2, :], in0=Ur[:rows, j % RING, :], in1=x1c[:rows, :], scale=1.0,
                                             scalar=0.0, op0=ALU.mult, op1=ALU.add, accum_out=acts[:rows, j:j + 1])\
                       .then_inc(sem("dot_done"), 1)
                if r:
                    diagonals(r - 1)
            diagonals(GR // 2 - 1)

        def dve_finish(dve, step, t, rows):
            wait(dve, "y_out3", 16 * t + 16)
            wait(dve, "vsum_done", NK * t + NK + RING)
            for e in range(2):
                ins = dve.scalar_tensor_tensor(out=y[:rows, 512 * e:512 * e + 512], in0=x1c[:rows, 512 * e:512 * e + 512],
                                               scalar=ALPHA, in1=bank[6 + e][:rows, :], op0=ALU.mult, op1=ALU.add)
            step(ins)
            layer_norm(dve, step, y, rows, 2, bn2, mv2, 18, "var2_ready", "sd2_ready", t + 1).then_inc(sem("y_ready"), 1)

        def slots(attention, output, head, combine, t, rows, sample):
            def slot(s):
                if sample is None:
                    if s < 4:
                        attention(t, s)
                else:
                    for b in ((0, 1), (2, 3), (4, 5), (6, 7))[s] if s < 4 else ():
                        sample(b)
                if s == 4:
                    output(t, rows)
                    head(t, 0, rows)
                    head(t, 1, rows)
                if s >= 5:
                    for e in range(2 * s - 8, 2 * s - 6):
                        head(t, e, rows)
                if s == 7 and combine is not None:
                    combine(t, rows)
            return slot

        with nc.Block() as block:

            @block.sync
            def _(sp):
                sp.dma_start(Ef.rearrange("p (n d) -> p n d", n=2 * EH), a["peer_sub_keys"][0].rearrange("e c n d -> n (e c) d"))\
                  .then_inc(sem("keys_in"), 16)
                with nc.allow_non_contiguous_dma(reason="1 KB in all"):
                    sp.dma_start(gk[:, :], a["peer_q_g"][0].rearrange("(c d) -> d c", c=2)).then_inc(sem("keys_in"), 16)
                sp.dma_start(subg[:, :], a["attn_subln_g"][0, :].partition_broadcast(P)).then_inc(sem("keys_in"), 16)
                sp.dma_start(w_out[:, :, :], a["w_out"][0].rearrange("(k p) n -> p k n", p=P)).then_inc(sem("w_out_in"), 16)
                for n, name in enumerate(("ln1_g", "ln1_b", "ln2_g", "ln2_b")):
                    sp.dma_start(lng[:, n, :], a[name][0, :].partition_broadcast(P)).then_inc(sem("ln_in"), 16)
                sp_front(sp, 0, P)
                with sp.Fori(0, NT - 1) as t:
                    sp_front(sp, t + 1, P)
                    sp_store(sp, t, P)
                sp_front(sp, NT, SR)
                sp_store(sp, NT - 1, P)
                sp_store(sp, NT, SR)
                sp.wait_ge(sem("y_out3"), 16 * (NT + 2))

            @block.gpsimd
            def _(pool):
                pool.iota(dist[:, :].bitcast(I32), [[1, SEQ]], base=0, channel_multiplier=-1).then_inc(sem("iota"), 1)
                pool.iota(iot_i[:, :], [[1, TOP]], base=0, channel_multiplier=0).then_inc(sem("iota"), 1)
                pool.iota(rowi[:, :], [[0, 2]], base=0, channel_multiplier=1).then_inc(sem("iota"), 1)
                pool.memset(qbd[:, :, :], 0.0).then_inc(sem("iota"), 1)
                pool.dma_start(pidx[:, :].bitcast(I32), a["page_table"].rearrange("b g -> (b g)").partition_broadcast(P))\
                    .then_inc(sem("pages_in"), 16)
                pool.iota(key[:, 0, 0:1].bitcast(I32), [[0, 1]], base=0, channel_multiplier=1).then_inc(sem("iota"), 1)
                pool.sem_inc(sem("dot_done"), RING)
                pool.sem_inc(sem("vsum_done"), RING)

                def experts(t, rows):
                    wait(pool, "cur_ready", t + 1, hold="pool")
                    with pool.Fori(0, EH) as e:
                        for b in range(2):
                            pool_group(pool, t, 2 * e + b, rows, b)

                with pool.Fori(0, NT - 1) as t:
                    experts(t, P)
                wait(pool, "cur_ready", NT)
                wait(pool, "map_ready", 4 * NT)
                pool.iota(coli, [[1, SEQ]], base=0, channel_multiplier=0).then_inc(sem("s_iota"), 1)
                wait(pool, "q_ps", EH * NT)
                for s in range(EH):
                    if s < 4:
                        pool_sample(pool, 2 * s)
                        pool_sample(pool, 2 * s + 1)
                    for b in range(2):
                        pool_group(pool, NT - 1, 2 * s + b, P, b)
                experts(NT, SR)

            @block.tensor
            def _(pe):
                pe.wait_ge(sem("keys_in"), 48)
                for n in range(2 * EH):
                    last = pe.transpose(bank[n // 4][:, n % 4 * P:(n % 4 + 1) * P], Ef[:, n * P:(n + 1) * P], ident[:, :])
                last.then_inc(sem("keys_ps"), 1)
                pe.wait_ge(sem("keys_ready"), 1)
                pe.wait_ge(sem("w_out_in"), 16)

                def front(t, rows, sample=None):
                    return slots(lambda t, h: pe_attention(pe, t, h), lambda t, r: pe_output(pe, t, r),
                                 lambda t, e, r: pe_head(pe, t, e, r), None, t, rows, sample)

                def experts(t, s, rows):
                    if s == 0:
                        wait(pe, "cur_ready", t + 1, hold="pe")
                        pe_group(pe, t, 0, rows, first=True)
                        pe_group(pe, t, 1, rows)
                    elif s == EH - 1:
                        pe_group(pe, t, 2 * s, rows)
                        pe_group(pe, t, 2 * s + 1, rows, last=True)
                    else:
                        with pe.Fori(2 * s, 2 * s + 2) as g:
                            pe_group(pe, t, g, rows)

                slot = front(0, P)
                for s in range(8):
                    slot(s)
                with pe.Fori(0, NT - 1) as t:
                    slot = front(t + 1, P)
                    for s in range(8):
                        slot(s)
                        experts(t, s, P)
                slot = front(NT, SR, lambda b: pe_sample(pe, b))
                for s in range(8):
                    slot(s)
                    experts(NT - 1, s, P)
                for s in range(8):
                    experts(NT, s, SR)

            @block.scalar
            def _(act):
                def front(t, rows, sample=None):
                    return slots(lambda t, h: act_attention(act, t, h), lambda t, r: act_output(act, t, r),
                                 lambda t, e, r: act_head(act, t, e, r), lambda t, r: act_combine(act, t, r), t, rows, sample)

                def experts(t, s, rows):
                    with act.Fori(2 * s, 2 * s + 2) as g:
                        act_group(act, t, g, rows)

                slot = front(0, P)
                for s in range(8):
                    slot(s)
                with act.Fori(0, NT - 1) as t:
                    slot = front(t + 1, P)
                    for s in range(8):
                        slot(s)
                        experts(t, s, P)
                    act_finish(act, t, P)
                slot = front(NT, SR, lambda b: act_sample(act, b))
                for s in range(8):
                    slot(s)
                    experts(NT - 1, s, P)
                act_finish(act, NT - 1, P)
                for s in range(8):
                    experts(NT, s, SR)
                act_finish(act, NT, SR)

            @block.vector
            def _(dve):
                step = Steps(dve, sem("dve_step3"))
                dve.wait_ge(sem("keys_in"), 48)
                dve.wait_ge(sem("iota"), 5)
                dve.wait_ge(sem("pages_in"), 16)
                step(dve.tensor_copy(bias[:, 0:SEQ], dist[:, :].bitcast(I32)))
                step(dve.tensor_copy(dist[:, :], bias[:, 0:SEQ]))
                step(dve.tensor_copy(iot[:, :], iot_i[:, :]))
                step(dve.tensor_scalar(subg[:, :], subg[:, :], 1.0 - LAM_INIT, None, ALU.mult))
                dve.wait_ge(sem("keys_ps"), 1)
                for n in range(2 * EH):
                    ins = dve.tensor_scalar(keysT[:, n, :], bank[n // 4][:, n % 4 * P:(n % 4 + 1) * P],
                                            gk[:, n % 2:n % 2 + 1], None, ALU.mult)
                step(ins)
                dve.sem_inc(sem("keys_ready"), 1)
                step(dve.tensor_copy(pf[:, 0:1], key[:, 0, 0:1].bitcast(I32)))
                step(dve.tensor_copy(gcur[:, 0:DB * PG], pidx[:, :].bitcast(I32)))
                step(dve.tensor_scalar(gcur[:, 0:DB * PG], gcur[:, 0:DB * PG], float(P), pf[:, 0:1], ALU.mult, ALU.add))
                step(dve.tensor_copy(pidx[:, :], gcur[:, 0:DB * PG]))
                q, slope, mw, hf, cf, rf = (rowc[:, n:n + 1] for n in range(6))
                step(dve.tensor_copy(rf, rowi[:, 0:1]))
                for dst, sh, mask in ((q, 0, DS - 1), (cf, 3, 1), (hf, 4, H - 1)):
                    step(dve.tensor_scalar(rowi[:, 1:2], rowi[:, 0:1], sh, mask, ALU.arith_shift_right, ALU.bitwise_and))
                    step(dve.tensor_copy(dst, rowi[:, 1:2]))
                step(dve.tensor_scalar(mw, neglam[0:64, :], -1.0, None, ALU.add))
                step(dve.tensor_scalar(mw, mw, cf, 1.0, ALU.mult, ALU.add))
                step(dve.tensor_scalar(headm[:, :], iot[0:64, 0:H], hf, None, ALU.is_equal))
                step(dve.tensor_scalar(slope, headm[:, 0:1], SLOPE[0], None, ALU.mult))
                for h in range(1, H):
                    step(dve.scalar_tensor_tensor(out=slope, in0=headm[:, h:h + 1], scalar=SLOPE[h], in1=slope,
                                                  op0=ALU.mult, op1=ALU.add))
                step(dve.memset(sel[:, :], 0.0))
                step(dve.tensor_scalar(sel[:, 56:56 + DS], iot[0:64, 0:DS], q, None, ALU.is_equal))
                dve.wait_ge(sem("ln_in"), 64)
                dve.sem_inc(sem("y_out3"), 16)

                def front(t, rows, sample=None):
                    return slots(lambda t, h: dve_attention(dve, step, t, h), lambda t, r: dve_output(dve, step, t, r),
                                 lambda t, e, r: dve_head(dve, step, t, e, r), lambda t, r: dve_combine(dve, step, t, r),
                                 t, rows, sample)

                def experts(t, s, rows):
                    with dve.Fori(2 * s, 2 * s + 2) as g:
                        dve_group(dve, t, g, rows)

                slot = front(0, P)
                for s in range(8):
                    slot(s)
                with dve.Fori(0, NT - 1) as t:
                    step.restart()
                    dve_begin(dve, step, t, P)
                    slot = front(t + 1, P)
                    for s in range(8):
                        slot(s)
                        experts(t, s, P)
                    dve_finish(dve, step, t, P)
                step.restart()
                dve_begin(dve, step, NT - 1, P)
                dve_sample_setup(dve, step)
                slot = front(NT, SR, lambda b: dve_sample(dve, step, b))
                for s in range(8):
                    slot(s)
                    experts(NT - 1, s, P)
                dve_finish(dve, step, NT - 1, P)
                dve_begin(dve, step, NT, SR)
                for s in range(8):
                    experts(NT, s, SR)
                dve_finish(dve, step, NT, SR)


_INS = ["x_all", "cache_k", "cache_v", "state_ssm_re", "state_ssm_im", "page_table", "w_in",
        "lambda_q1", "lambda_k1", "lambda_q2", "lambda_k2", "attn_subln_g", "ssm_lambda_re", "ssm_lambda_im",
        "ssm_log_dt", "ssm_b_re", "ssm_b_im", "ssm_c_re", "ssm_c_im", "ssm_d", "ssm_w_glu", "ssm_b_glu",
        "w_out", "ln1_g", "ln1_b", "peer_w_q", "peer_q_g", "peer_sub_keys", "peer_u", "peer_v", "ln2_g", "ln2_b"]
_OUTS = [(1, SEQ, DM), (DB, DS, DM), (1, 1, SEQ, H, 2, DQ), (1, 1, SEQ, H, DV), (1, 1, G, SP_), (1, 1, G, SP_),
         (1, DB, DS, H, 2, DQ), (1, DB, DS, H, DV), (1, DB, G, SP_), (1, DB, G, SP_)]


def kernel(**inputs):
    import numpy as _np
    import concourse.bacc as _bacc
    from concourse import mybir as _mybir
    from concourse.bass_utils import run_bass_kernel_spmd as _run

    nc = _bacc.Bacc("TRN2", target_bir_lowering=False, num_devices=1)
    data = {n: _np.ascontiguousarray(v) for n, v in inputs.items()}
    xp, xs = data.pop("x_prompt"), data.pop("x_sample")
    data["x_all"] = _np.concatenate([xp.reshape(SEQ, DM), xs.reshape(SR, DM), _np.zeros((P - SR, DM), xp.dtype)])
    arrays, ins = {}, {}
    for n in _INS:
        arrays[f"in_{n}"] = data[n]
        ins[n] = nc.dram_tensor(f"in_{n}", data[n].shape, _mybir.dt.from_np(data[n].dtype), kind="ExternalInput").ap()
    outs = [nc.dram_tensor(f"out_{i}", shape, _mybir.dt.float32, kind="ExternalOutput").ap()
            for i, shape in enumerate(_OUTS)]
    build(nc, ins, outs)
    r = _run(nc, [arrays], core_ids=[0])
    return tuple(r.results[0][f"out_{i}"] for i in range(len(_OUTS)))
```

```python
import math
from contextlib import ExitStack

import numpy as np
import concourse.bass as bass
from concourse import mybir
from concourse.alu_op_type import AluOpType as ALU

F32 = mybir.dt.float32
I32 = mybir.dt.int32
U32 = mybir.dt.uint32
ACT = mybir.ActivationFunctionType
X = mybir.AxisListType.X

P = 128
DM = 1024
KC = DM // P
SEQ = 1024
NT = SEQ // P
DB, DS = 8, 8
SR = DB * DS
TP = SEQ + P
DA = 512
H = 4
DQ = 64
DV = 128
G, C, SP_ = 32, 16, 64
GP = G // 2
L = 8
NCH = SEQ // L
NC = NCH + DB
PAST = 1024
PG = 8
EH = 8
TOP = 16
NK = EH * TOP
NKEY = 128
EPS = 1e-5
ALPHA = 2.0 ** 0.25
LAM_INIT = 0.8 - 0.6 * math.exp(0.0)
SLOPE = [2.0 ** (-8.0 * (h + 1) / H) for h in range(H)]
QSCALE = [DQ ** -0.5 / s for s in SLOPE]
MASKED = -1e34
LOW = -3.0e38
WB = SEQ - P
RING = 4

PI2A = 6.28125
PI2B = 0.0019350051879882812
PI2C = 2 * math.pi - PI2A - PI2B
MAGIC = 12582912.0


class Steps:

    def __init__(self, eng, sem):
        self.eng, self.sem, self.n = eng, sem, 0

    def __call__(self, ins):
        self.n += 1
        ins.then_inc(self.sem, 1)
        self.eng.wait_ge(self.sem, self.n)

    def restart(self):
        self.eng.sem_clear(self.sem)
        self.n = 0


def build(nc, a, o):
    top = ExitStack()
    with top:
        def alloc(ctx):
            def sb(name, shape, dt=F32):
                return ctx.enter_context(nc.sbuf_tensor(name, shape, dt))
            return sb

        sems = {}

        def sem(name):
            if name not in sems:
                sems[name] = top.enter_context(nc.semaphore(name))
            return sems[name]

        sb = alloc(top)
        ident = sb("ident", [P, P])
        zero = sb("zero", [P, 1])
        kT = sb("kT", [P, H, TP])
        vrows = sb("vrows", [P, NT + 1, DA])
        neglam = sb("neglam", [P, 1])
        psum = top.enter_context(nc.psum_tensor("psum", [P, 8, 512], F32))
        bank = [psum[:, i, :] for i in range(8)]

        scr_q = nc.dram_tensor("scr_q", (P, H, TP), F32, kind="Internal").ap()
        scr_s = nc.dram_tensor("scr_s", (P, H, TP), F32, kind="Internal").ap()
        scr_u = nc.dram_tensor("scr_u", (G, C, L, NC), F32, kind="Internal").ap()
        scr_y = nc.dram_tensor("scr_y", (G, C, L, NC), F32, kind="Internal").ap()

        projections(nc, a, o, alloc, sem, ident, zero, kT, vrows, neglam, bank, scr_q, scr_u)
        state_space(nc, a, o, alloc, sem, ident, bank, scr_u, scr_y, scr_s)
        trunk(nc, a, o, alloc, sem, ident, kT, vrows, neglam, bank, psum, scr_q, scr_s)


def projections(nc, a, o, alloc, sem, ident, zero, kT, vrows, neglam, bank, scr_q, scr_u):
    with ExitStack() as ctx:
        sb = alloc(ctx)
        w = sb("w_in_sb", [P, KC, 4 * DA])
        xr = sb("xr", [P, 2, DM])
        xT = sb("xT", [P, KC, P])
        qrow = sb("qrow", [P, DA])
        krow = sb("krow", [P, DA])
        urow = sb("urow", [P, DA])
        qTs = sb("qTs", [P, H, P])
        uT = sb("uT", [P, 4, L, TP // L])
        lamv = sb("lamv", [P, 4, DQ])
        lamw = sb("lamw", [P, DQ])
        lams = sb("lams", [P, 4])
        k_rows = o[2].rearrange("d b t h c q -> (d b t) (h c q)")
        v_rows = o[3].rearrange("d b t h v -> (d b t) (h v)")
        ks_rows = o[6].rearrange("d b t h c q -> (d b t) (h c q)")
        vs_rows = o[7].rearrange("d b t h v -> (d b t) (h v)")
        x_rows = a["x_all"]
        w_v = a["w_in"].rearrange("o (k p) n -> p (o k) n", p=P)

        with nc.Block() as block:

            @block.sync
            def _(sp):
                for n, name in enumerate(("lambda_q1", "lambda_k1", "lambda_q2", "lambda_k2")):
                    sp.dma_start(lamv[:, n, :], a[name][0, :].partition_broadcast(P)).then_inc(sem("lam_in"), 16)
                for s in range(2):
                    sp.dma_start(xr[:, s, :], x_rows[s * P:(s + 1) * P, :]).then_inc(sem(f"x_in{s}"), 16)
                for g in range(4):
                    sp.dma_start(w[:, :, g * DA:(g + 1) * DA], w_v[:, :, g * DA:(g + 1) * DA])\
                        .then_inc(sem(f"w_in{g}"), 16)
                with sp.Fori(0, NT // 2 - 1) as i:
                    for s in range(2):
                        sp.wait_ge(sem("p_xTps"), 2 * i + s + 1)
                        sp.dma_start(xr[:, s, :], x_rows[bass.ds(i * 2 * P + (2 + s) * P, P), :])\
                          .then_inc(sem(f"x_in{s}"), 16)
                sp.wait_ge(sem("p_xTps"), NT - 1)
                sp.dma_start(xr[:, 0, :], x_rows[NT * P:(NT + 1) * P, :]).then_inc(sem("x_in0"), 16)

            @block.gpsimd
            def _(pool):
                pool.memset(ident[:, :], 0.0).then_inc(sem("id0"), 1)
                pool.memset(zero[:, :], 0.0)
                pool.wait_ge(sem("id0"), 1)
                pool.affine_select(out=ident[:, :], in_=ident[:, :], compare_op=ALU.not_equal, fill=1.0,
                                   base=0, pattern=[[-1, P]], channel_multiplier=1).then_inc(sem("ident"), 1)

            @block.tensor
            def _(pe):
                pe.wait_ge(sem("ident"), 1)

                def tile(i, s):
                    t = 2 * i + s
                    pe.wait_ge(sem(f"x_in{s}"), 16 * i + 16)
                    for k in range(KC):
                        last = pe.transpose(bank[4 + k // 4][:, (k % 4) * P:(k % 4 + 1) * P],
                                            xr[:, s, k * P:(k + 1) * P], ident[:, :])
                    last.then_inc(sem("p_xTps"), 1)
                    pe.wait_ge(sem("p_xT"), t + 1)
                    for g in range(4):
                        pe.wait_ge(sem(f"w_in{g}"), 16)
                        for k in range(KC):
                            last = pe.matmul(bank[g][:, :], xT[:, k, :], w[:, k, g * DA:(g + 1) * DA],
                                             start=k == 0, stop=k == KC - 1)
                        last.then_inc(sem("p_z"), 1)
                    for g, row, b in ((0, qrow, 6), (1, krow, 7), (3, urow, 4)):
                        pe.wait_ge(sem(("p_qrow", "p_krow", None, "p_urow")[g]), t + 1)
                        for h in range(4):
                            last = pe.transpose(bank[b][:, h * P:(h + 1) * P], row[:, h * P:(h + 1) * P], ident[:, :])
                        last.then_inc(sem("p_T"), 1)
                    pe.wait_ge(sem("p_Tcopied"), 3 * t + 3)
                    pe.wait_ge(sem("p_vrow"), t + 1)

                with pe.Fori(0, NT // 2) as i:
                    tile(i, 0)
                    tile(i, 1)
                tile(NT // 2, 0)

            @block.vector
            def _(dve):
                step = Steps(dve, sem("dve_step"))
                dve.wait_ge(sem("lam_in"), 64)
                for n in range(2):
                    step(dve.tensor_tensor_reduce(out=lamw[:, :], in0=lamv[:, 2 * n, :], in1=lamv[:, 2 * n + 1, :],
                                                  scale=1.0, scalar=0.0, op0=ALU.mult, op1=ALU.add,
                                                  accum_out=lams[:, n:n + 1]))
                dve.sem_inc(sem("lam_dots"), 1)
                dve.wait_ge(sem("lam_exp"), 1)
                step(dve.tensor_tensor(lams[:, 0:1], lams[:, 3:4], lams[:, 2:3], ALU.subtract))
                step(dve.tensor_scalar(neglam[:, :], lams[:, 0:1], -LAM_INIT, None, ALU.add))

                def tile(t, tk):
                    dve.wait_ge(sem("p_xTps"), t + 1)
                    for b in range(2):
                        last = dve.tensor_copy(xT[:, 4 * b:4 * b + 4, :].rearrange("p k t -> p (k t)"), bank[4 + b][:, :])
                    last.then_inc(sem("p_xT"), 1)
                    dve.wait_ge(sem("p_z"), 4 * t + 1)
                    for h in range(H):
                        last = dve.tensor_scalar(qrow[:, h * P:(h + 1) * P], bank[0][:, h * P:(h + 1) * P],
                                                 QSCALE[h], None, ALU.mult)
                    last.then_inc(sem("p_qrow"), 1)
                    dve.wait_ge(sem("p_z"), 4 * t + 4)
                    dve.tensor_copy(urow[:, :], bank[3][:, :]).then_inc(sem("p_urow"), 1)
                    dve.wait_ge(sem("p_T"), 3 * t + 1)
                    dve.wait_ge(sem("q_out"), 16 * t + 16)
                    dve.tensor_copy(qTs[:, :, :].rearrange("p h t -> p (h t)"), bank[6][:, :])\
                       .then_inc(sem("p_Tcopied"), 1)
                    dve.sem_inc(sem("p_qTs"), 1)
                    dve.wait_ge(sem("p_T"), 3 * t + 2)
                    dve.tensor_copy(kT[:, :, bass.ds(tk * P, P)], bank[7][:, :].rearrange("p (h t) -> p h t", h=H))\
                       .then_inc(sem("p_Tcopied"), 1)
                    dve.wait_ge(sem("p_T"), 3 * t + 3)
                    for q in range(4):
                        last = dve.tensor_copy(uT[:, q, :, bass.ds(tk * (P // L), P // L)],
                                               bank[4][:, q * P:(q + 1) * P].rearrange("p (n j) -> p j n", j=L))
                    last.then_inc(sem("p_Tcopied"), 1)

                dve.sem_inc(sem("q_out"), 16)
                with dve.Fori(0, NT + 1) as t:
                    tile(t, t)

            @block.scalar
            def _(act):
                act.wait_ge(sem("lam_dots"), 1)
                act.activation(lams[:, 2:4], lams[:, 0:2], ACT.Exp).then_inc(sem("lam_exp"), 1)

                def tile(t, rows, kdst, vdst):
                    act.wait_ge(sem("p_z"), 4 * t + 2)
                    act.wait_ge(sem("k_out"), 16 * t + 16)
                    act.activation(krow[:, :], bank[1][:, :], ACT.Copy).then_inc(sem("p_krow"), 1)
                    act.wait_ge(sem("p_z"), 4 * t + 3)
                    act.activation(vrows[:, bass.ds(t, 1), :].rearrange("p o n -> p (o n)"), bank[2][:, :], ACT.Copy)\
                       .then_inc(sem("p_vrow"), 1)
                    act.wait_ge(sem("p_krow"), t + 1)
                    act.dma_start(kdst, krow[:rows, :]).then_inc(sem("k_out"), 16)
                    act.wait_ge(sem("p_vrow"), t + 1)
                    act.dma_start(vdst, vrows[:rows, bass.ds(t, 1), :].rearrange("p o n -> p (o n)"))\
                       .then_inc(sem("v_out"), 16)
                    act.wait_ge(sem("p_Tcopied"), 3 * t + 1)
                    act.wait_ge(sem("p_qTs"), t + 1)
                    act.dma_start(scr_q[:, :, bass.ds(t * P, P)], qTs[:, :, :]).then_inc(sem("q_out"), 16)

                act.sem_inc(sem("k_out"), 16)
                with act.Fori(0, NT) as t:
                    tile(t, P, k_rows[bass.ds(t * P, P), :], v_rows[bass.ds(t * P, P), :])
                tile(NT, SR, ks_rows, vs_rows)
                act.wait_ge(sem("p_Tcopied"), 3 * (NT + 1))
                for q in range(4):
                    act.dma_start(scr_u[8 * q:8 * q + 8, :, :, :].rearrange("g c j n -> (g c) j n"),
                                  uT[:, q, :, 0:NC]).then_inc(sem("u_out"), 16)
                act.wait_ge(sem("k_out"), 16 * (NT + 2))
                act.wait_ge(sem("v_out"), 16 * (NT + 1))
                act.wait_ge(sem("q_out"), 16 * (NT + 2))
                act.wait_ge(sem("u_out"), 64)


def state_space(nc, a, o, alloc, sem, ident, bank, scr_u, scr_y, scr_s):
    with ExitStack() as ctx:
        sb = alloc(ctx)
        U = sb("U", [P, G, NC])
        prow = sb("prow", [GP, 4, P])
        dtg = sb("dtg", [GP, 2])
        pcol = sb("pcol", [P, 4, GP])
        hrow = sb("hrow", [P, 2, P])
        crow = sb("crow", [P, 2, 2, 2, SP_])
        B = sb("B", [P, 2, GP, C])
        BB = sb("BB", [P, 2, GP, C])
        Cc = sb("Cc", [P, 2, GP, C])
        h0 = sb("h0", [P, 2, DB, GP])
        s1 = sb("s1", [P, 24, GP])
        pw = sb("pw", [P, 2, L + 1, GP])
        CP = sb("CP", [P, 2, GP, L + 1, C])
        BP = sb("BP", [P, 2, GP, L, C])
        W = sb("W", [P, GP, 2, 192])
        T = sb("T", [P, G, P])
        dcol = sb("dcol", [C, G])
        EX = sb("EX", [P, 2, GP, NCH])
        K0 = EX[0:C, :, :, :].rearrange("c n i k -> c (n i k)").rearrange("c (g m d) -> c g m d", g=G, m=L)
        V = sb("V", [P, 2, GP, NC])
        R8 = sb("R8", [P, GP, NCH])
        HP = W[:, :, :, :].rearrange("p i n c -> p (i n c)")[:, 0:2 * GP * NC]\
            .rearrange("p (n i c) -> p n i c", n=2, i=GP)
        tA = sb("tA", [P, GP * NCH])
        tB = sb("tB", [P, GP * NCH])
        hout = sb("hout", [P, 4, P])

        with nc.Block() as block:
            @block.sync
            def _(sp):
                for n, name in enumerate(("ssm_lambda_re", "ssm_lambda_im")):
                    sp.dma_start(prow[:, n, :], a[name][0].rearrange("(i g) p -> i (g p)", g=2)).then_inc(sem("ss_in"), 16)
                sp.dma_start(dtg[:, :], a["ssm_log_dt"][0].rearrange("(i g) -> i g", g=2)).then_inc(sem("ss_in"), 16)
                for n, name in enumerate(("ssm_b_re", "ssm_b_im")):
                    sp.dma_start(B[:, n, :, :], a[name][0].rearrange("(i g) p c -> (g p) i c", g=2)).then_inc(sem("ss_in"), 16)
                for n, name in enumerate(("ssm_c_re", "ssm_c_im")):
                    for e in range(2):
                        for i in range(8):
                            sp.dma_start(crow[C * i:C * i + C, n, e, :, :],
                                         a[name][0, 16 * e + 2 * i:16 * e + 2 * i + 2, :, :].rearrange("g c p -> c g p"))\
                              .then_inc(sem("ss_in"), 16)
                for n, name in enumerate(("state_ssm_re", "state_ssm_im")):
                    sp.dma_start(hrow[:, n, :], a[name][0].rearrange("b (i g) p -> (b i) (g p)", g=2)).then_inc(sem("ss_in"), 16)
                with nc.allow_non_contiguous_dma(reason="2 KB in all"):
                    sp.dma_start(dcol[:, :], a["ssm_d"][0].rearrange("g c -> c g")).then_inc(sem("ss_in"), 16)
                for j in range(L):
                    sp.dma_start(U[C * j:C * j + C, :, :], scr_u[:, :, j, :].rearrange("g c n -> c g n"))\
                      .then_inc(sem("U_in"), 16)
                sp.wait_ge(sem("ss_K0"), 1)
                for j in range(L):
                    sp.dma_start(T[C * j:C * j + C, :, C * j:P],
                                 K0[:, :, 0:L - j, :].rearrange("c g m d -> c g (m d)")).then_inc(sem("T_in"), 16)
                sp.wait_ge(sem("T_in"), 16 * L)
                sp.wait_ge(sem("ss_y"), GP // 3 + 1)
                for j in range(L):
                    sp.dma_start(scr_y[:, :, j, :].rearrange("g c n -> c g n"), U[C * j:C * j + C, :, :])\
                      .then_inc(sem("y_out"), 16)
                sp.wait_ge(sem("y_out"), 16 * L)
                sp.wait_ge(sem("ss_hout"), 1)
                for n in range(2):
                    sp.dma_start(o[4 + n].rearrange("d b (i g) p -> (d b i) (g p)", g=2), hout[0:GP, n, :])\
                      .then_inc(sem("h_out"), 16)
                    sp.dma_start(o[8 + n].rearrange("d b (i g) p -> (d b i) (g p)", g=2), hout[:, 2 + n, :])\
                      .then_inc(sem("h_out"), 16)
                sp.wait_ge(sem("h_out"), 64)

            @block.gpsimd
            def _(pool):
                pool.memset(T[:, :, :], 0.0).then_inc(sem("T_zero"), 1)
                pool.memset(W[:, :, :, 64:128], 0.0).then_inc(sem("W_zero"), 1)

            @block.tensor
            def _(pe):
                pe.wait_ge(sem("ss_prow"), 1)
                for n in range(3):
                    last = pe.transpose(bank[0][:, n * GP:(n + 1) * GP], prow[:, n, :], ident[:GP, :GP])
                for n in range(2):
                    last = pe.transpose(bank[1][:, n * P:(n + 1) * P], hrow[:, n, :], ident[:, :])
                for n in range(2):
                    for e in range(2):
                        last = pe.transpose(bank[2][:, (2 * n + e) * P:(2 * n + e + 1) * P],
                                            crow[:, n, e, :, :].rearrange("p g s -> p (g s)"), ident[:, :])
                last.then_inc(sem("ss_cols"), 1)
                pe.wait_ge(sem("ss_BP"), 1)
                for r in range(8):
                    if r >= 2:
                        pe.wait_ge(sem("ss_Wcopied"), r - 1)
                    for q in range(4):
                        n, i = divmod(4 * r + q, GP)
                        last = pe.transpose(bank[r % 2][:, q * P:(q + 1) * P],
                                            BP[:, n, i, :, :].rearrange("p j c -> p (j c)"), ident[:, :])
                    last.then_inc(sem("ss_Wps"), 1)
                pe.wait_ge(sem("ss_CP"), 1)
                for r in range(4):
                    if r >= 2:
                        pe.wait_ge(sem("ss_Kcopied"), r - 1)
                    for g in range(8 * r, 8 * r + 8):
                        i, s = g // 2, g % 2 * 64
                        for n in range(2):
                            last = pe.matmul(bank[2 + 4 * (r % 2) + g % 2][0:C, i % 4 * P:(i % 4 + 1) * P],
                                             BB[s:s + 64, n, i, :],
                                             CP[s:s + 64, n, i, 0:L, :].rearrange("p m c -> p (m c)"),
                                             start=n == 0, stop=n == 1)
                    last.then_inc(sem("ss_Kps"), 1)
                pe.wait_ge(sem("ss_Wcopied"), 8)
                pe.wait_ge(sem("U_in"), 16 * L)
                for i in range(GP):
                    if i >= 2:
                        pe.wait_ge(sem("ss_Vcopied"), i - 1)
                    for n in range(2):
                        for s in range(2):
                            last = pe.matmul(bank[4 + i % 2][:, n * NC:(n + 1) * NC], W[:, i, n, 64 * s:64 * s + P],
                                             U[:, 2 * i + s, :], start=s == 0, stop=s == 1)
                    last.then_inc(sem("ss_Vps"), 1)
                pe.wait_ge(sem("T_in"), 16 * L)
                pe.wait_ge(sem("ss_HP"), 1)
                for g in range(G):
                    i, s = g // 2, g % 2 * 64
                    r, q = divmod(i, 3)
                    if q == 0 and s == 0:
                        pe.wait_ge(sem("ss_Kcopied"), 4)
                        if r >= 2:
                            pe.wait_ge(sem("ss_y"), r - 1)
                    out = bank[(2, 6)[r % 2] + g % 2][:, q * NC:(q + 1) * NC]
                    pe.matmul(out, T[:, g, :], U[:, g, :], start=True, stop=False)
                    for n in range(2):
                        last = pe.matmul(out, CP[s:s + 64, n, i, 1:L + 1, :].rearrange("p m c -> p (m c)"),
                                         HP[s:s + 64, n, i, :], start=False, stop=n == 1)
                    if s and (q == 2 or g == G - 1):
                        last.then_inc(sem("ss_yps"), 1)
                pe.wait_ge(sem("ss_hs"), 1)
                for n in range(2):
                    pe.transpose(bank[0][0:GP, n * P:(n + 1) * P], s1[:, 20 + n, :], ident[:, :])
                for n in range(2):
                    last = pe.transpose(bank[1][:, n * P:(n + 1) * P],
                                        tA[:, n * P:(n + 1) * P], ident[:, :])
                last.then_inc(sem("ss_hps"), 1)

            @block.scalar
            def _(act):
                act.wait_ge(sem("ss_arg"), 1)
                act.activation(s1[:, 3, :], s1[:, 2, :], ACT.Exp).then_inc(sem("ss_dt"), 1)
                act.wait_ge(sem("ss_arg"), 2)
                act.activation(s1[:, 5, :], s1[:, 4, :], ACT.Exp).then_inc(sem("ss_mag"), 1)
                act.wait_ge(sem("ss_arg"), 3)
                act.activation(s1[:, 8, :], s1[:, 7, :], ACT.Sin)
                act.activation(s1[:, 9, :], s1[:, 7, :], ACT.Sin, scale=0.5).then_inc(sem("ss_sin"), 1)
                for r in range(8):
                    act.wait_ge(sem("ss_Wps"), r + 1)
                    if r == 0:
                        act.wait_ge(sem("W_zero"), 1)
                    n, i = divmod(4 * r, GP)
                    for s in range(2):
                        last = act.activation(W[:, i:i + 4, n, 128 * s:128 * s + 64],
                                              bank[r % 2][:, :].rearrange("p (q s c) -> p q s c", q=4, s=2)[:, :, s, :],
                                              ACT.Copy)
                    last.then_inc(sem("ss_Wcopied"), 1)
                for i in range(GP):
                    act.wait_ge(sem("ss_Vps"), i + 1)
                    act.activation(V[:, :, i, :], bank[4 + i % 2][:, 0:2 * NC].rearrange("p (n c) -> p n c", n=2),
                                   ACT.Copy).then_inc(sem("ss_Vcopied"), 1)
                for r in range(GP // 3 + 1):
                    act.wait_ge(sem("ss_yps"), r + 1)
                    n = min(3, GP - 3 * r)
                    for q in range(2):
                        last = act.activation(U[:, 6 * r:6 * r + 2 * n, :].rearrange("p (i s) c -> p i s c", s=2)[:, :, q, :],
                                              bank[(2, 6)[r % 2] + q][:, 0:n * NC].rearrange("p (i c) -> p i c", i=n),
                                              ACT.Gelu)
                    last.then_inc(sem("ss_y"), 1)

            @block.vector
            def _(dve):
                step = Steps(dve, sem("dve_step2"))
                tt, ts = dve.tensor_tensor, dve.tensor_scalar

                def cmul(ore, oim, ar, ai, br, bi, shape, neg_im=False):
                    n = int(np.prod(shape))
                    names = " ".join("wxyz"[:len(shape)])
                    kw = dict(zip("wxyz", shape))
                    t1 = tA[:, 0:n].rearrange(f"p ({names}) -> p {names}", **kw)
                    t2 = tB[:, 0:n].rearrange(f"p ({names}) -> p {names}", **kw)
                    tt(t1, ar, br, ALU.mult)
                    step(tt(t2, ai, bi, ALU.mult))
                    step(tt(ore, t1, t2, ALU.subtract))
                    tt(t1, ar, bi, ALU.mult)
                    step(tt(t2, ai, br, ALU.mult))
                    if neg_im:
                        step(tt(t1, t1, t2, ALU.add))
                        step(ts(oim, t1, -1.0, None, ALU.mult))
                    else:
                        step(tt(oim, t1, t2, ALU.add))

                dve.wait_ge(sem("ss_in"), 16 * (3 + 2 + 32 + 2 + 1))
                for s in range(2):
                    last = dve.tensor_copy(prow[:, 2, s * 64:s * 64 + 64], dtg[:, s:s + 1].broadcast_to((GP, 64)))
                last.then_inc(sem("ss_prow"), 1)
                dve.wait_ge(sem("ss_cols"), 1)
                dve.tensor_copy(s1[:, 0:3, :].rearrange("p n i -> p (n i)"), bank[0][:, 0:3 * GP])
                dve.tensor_copy(h0[:, :, :, :].rearrange("p n b i -> p (n b i)"), bank[1][:, 0:2 * P])
                step(dve.tensor_copy(Cc[:, :, :, :].rearrange("p n i c -> p (n i c)"), bank[2][:, :]))
                dve.sem_inc(sem("ss_arg"), 1)
                lr, li, dt = s1[:, 0, :], s1[:, 1, :], s1[:, 3, :]
                dve.wait_ge(sem("ss_dt"), 1)
                step(tt(s1[:, 4, :], lr, dt, ALU.mult))
                dve.sem_inc(sem("ss_arg"), 1)
                step(tt(s1[:, 6, :], li, dt, ALU.mult))
                step(ts(s1[:, 10, :], s1[:, 6, :], 1.0 / (2 * math.pi), MAGIC, ALU.mult, ALU.add))
                step(ts(s1[:, 10, :], s1[:, 10, :], -MAGIC, None, ALU.add))
                step(dve.scalar_tensor_tensor(out=s1[:, 6, :], in0=s1[:, 10, :], scalar=-PI2A, in1=s1[:, 6, :],
                                              op0=ALU.mult, op1=ALU.add))
                step(dve.scalar_tensor_tensor(out=s1[:, 6, :], in0=s1[:, 10, :], scalar=-PI2B, in1=s1[:, 6, :],
                                              op0=ALU.mult, op1=ALU.add))
                step(dve.scalar_tensor_tensor(out=s1[:, 6, :], in0=s1[:, 10, :], scalar=-PI2C, in1=s1[:, 6, :],
                                              op0=ALU.mult, op1=ALU.add))
                step(ts(s1[:, 7, :], s1[:, 6, :], 3.1415925, -3.1415925, ALU.min, ALU.max))
                dve.sem_inc(sem("ss_arg"), 1)
                dve.wait_ge(sem("ss_mag"), 1)
                dve.wait_ge(sem("ss_sin"), 1)
                sin, mag = s1[:, 8, :], s1[:, 5, :]
                cos = s1[:, 9, :]
                step(tt(s1[:, 9, :], s1[:, 9, :], s1[:, 9, :], ALU.mult))
                step(ts(cos, s1[:, 9, :], -2.0, 1.0, ALU.mult, ALU.add))
                dve.memset(pw[:, 0, 0, :], 1.0)
                dve.memset(pw[:, 1, 0, :], 0.0)
                tt(pw[:, 0, 1, :], mag, cos, ALU.mult)
                step(tt(pw[:, 1, 1, :], mag, sin, ALU.mult))
                n = 1
                while n < L:
                    w_ = [pw[:, q, n:n + 1, :].broadcast_to((P, n, GP)) for q in range(2)]
                    cmul(pw[:, 0, n + 1:2 * n + 1, :], pw[:, 1, n + 1:2 * n + 1, :],
                         pw[:, 0, 1:n + 1, :], pw[:, 1, 1:n + 1, :], w_[0], w_[1], (n, GP))
                    n *= 2
                are, aim = pw[:, 0, 1, :], pw[:, 1, 1, :]
                nre, den, t3, t4 = s1[:, 11, :], s1[:, 12, :], s1[:, 13, :], s1[:, 14, :]
                gre, gim = s1[:, 15, :], s1[:, 16, :]
                ts(nre, are, -1.0, None, ALU.add)
                tt(t3, lr, lr, ALU.mult)
                step(tt(t4, li, li, ALU.mult))
                step(tt(den, t3, t4, ALU.add))
                step(dve.reciprocal(den, den))
                tt(t3, nre, lr, ALU.mult)
                step(tt(t4, aim, li, ALU.mult))
                step(tt(gre, t3, t4, ALU.add))
                step(tt(gre, gre, den, ALU.mult))
                tt(t3, aim, lr, ALU.mult)
                step(tt(t4, nre, li, ALU.mult))
                step(tt(gim, t3, t4, ALU.subtract))
                step(tt(gim, gim, den, ALU.mult))
                gb = [g_.rearrange("p (i o) -> p i o", o=1).broadcast_to((P, GP, C)) for g_ in (gre, gim)]
                cmul(BB[:, 0, :, :], BB[:, 1, :, :], gb[0], gb[1], B[:, 0, :, :], B[:, 1, :, :], (GP, C))
                for j in range(L):
                    pj = [pw[:, q, L - 1 - j, :].rearrange("p (i o) -> p i o", o=1).broadcast_to((P, GP, C)) for q in range(2)]
                    cmul(BP[:, 0, :, j, :], BP[:, 1, :, j, :], BB[:, 0, :, :], BB[:, 1, :, :], pj[0], pj[1], (GP, C))
                dve.sem_inc(sem("ss_BP"), 1)
                for m in range(L + 1):
                    pj = [pw[:, q, m, :].rearrange("p (i o) -> p i o", o=1).broadcast_to((P, GP, C)) for q in range(2)]
                    cmul(CP[:, 0, :, m, :], CP[:, 1, :, m, :], Cc[:, 0, :, :], Cc[:, 1, :, :], pj[0], pj[1], (GP, C),
                         neg_im=True)
                dve.sem_inc(sem("ss_CP"), 1)
                for r in range(4):
                    dve.wait_ge(sem("ss_Kps"), r + 1)
                    for q in range(2):
                        last = dve.tensor_copy(
                            K0[:, 8 * r:8 * r + 8, :, :].rearrange("p (i s) m c -> p i s (m c)", s=2)[:, :, q, :],
                            bank[2 + 4 * (r % 2) + q][0:C, :].rearrange("p (i x) -> p i x", i=4))
                    last.then_inc(sem("ss_Kcopied"), 1)
                dve.wait_ge(sem("ss_Kcopied"), 4)
                skip = tA[0:C, 0:G * C].rearrange("p (g c) -> p g c", c=C)
                step(tt(skip, dcol[:, :].rearrange("p (g o) -> p g o", o=1).broadcast_to((C, G, C)),
                        ident[0:C, 0:C].rearrange("p (o c) -> p o c", o=1).broadcast_to((C, G, C)), ALU.mult))
                step(tt(K0[:, :, 0, :], K0[:, :, 0, :], skip, ALU.add))
                dve.wait_ge(sem("T_zero"), 1)
                dve.sem_inc(sem("ss_K0"), 1)
                ur = [s1[:, 17, :], s1[:, 18, :]]
                r8 = s1[:, 19, :]
                dve.tensor_copy(ur[0], cos)
                dve.tensor_copy(r8, mag)
                step(dve.tensor_copy(ur[1], sin))
                for _ in range(3):
                    step(tt(r8, r8, r8, ALU.mult))
                    cmul(t3, t4, ur[0], ur[1], ur[0], ur[1], (GP,))
                    dve.tensor_copy(ur[0], t3)
                    step(dve.tensor_copy(ur[1], t4))
                dve.wait_ge(sem("T_in"), 16 * L)
                dve.memset(EX[:, 0, :, 0:1], 1.0)
                step(dve.memset(EX[:, 1, :, 0:1], 0.0))
                n = 1
                while n < NCH:
                    w_ = [u_.rearrange("p (i o) -> p i o", o=1).broadcast_to((P, GP, n)) for u_ in ur]
                    cmul(EX[:, 0, :, n:2 * n], EX[:, 1, :, n:2 * n], EX[:, 0, :, 0:n], EX[:, 1, :, 0:n],
                         w_[0], w_[1], (GP, n))
                    if 2 * n < NCH:
                        cmul(t3, t4, ur[0], ur[1], ur[0], ur[1], (GP,))
                        dve.tensor_copy(ur[0], t3)
                        step(dve.tensor_copy(ur[1], t4))
                    n *= 2
                step(dve.tensor_copy(R8[:, :, :], r8.rearrange("p (i o) -> p i o", o=1).broadcast_to((P, GP, NCH))))
                step(dve.memset(R8[:, :, 0:1], 0.0))
                dve.wait_ge(sem("ss_Vcopied"), GP)
                vr, vi = V[:, 0, :, 0:NCH], V[:, 1, :, 0:NCH]
                er, ei = EX[:, 0, :, :], EX[:, 1, :, :]
                t1 = tA[:, 0:GP * NCH].rearrange("p (i n) -> p i n", i=GP)
                t2 = tB[:, 0:GP * NCH].rearrange("p (i n) -> p i n", i=GP)
                zr = BP[:, 0, :, :, :].rearrange("p i j c -> p i (j c)")
                zi = BP[:, 1, :, :, :].rearrange("p i j c -> p i (j c)")
                tt(t1, vr, er, ALU.mult)
                step(tt(t2, vi, ei, ALU.mult))
                step(tt(zr, t1, t2, ALU.add))
                tt(t1, vi, er, ALU.mult)
                step(tt(t2, vr, ei, ALU.mult))
                step(tt(zi, t1, t2, ALU.subtract))
                for q, z in ((0, tA), (1, tB)):
                    step(dve.tensor_tensor_scan(z[:, 0:GP * NCH], R8[:, :, :].rearrange("p i n -> p (i n)"),
                                                BP[:, q, :, :, :].rearrange("p i j c -> p (i j c)"),
                                                0.0, ALU.mult, ALU.add))
                tt(zr, t1, er, ALU.mult)
                step(tt(zi, t2, ei, ALU.mult))
                step(tt(vr, zr, zi, ALU.subtract))
                tt(zr, t1, ei, ALU.mult)
                step(tt(zi, t2, er, ALU.mult))
                step(tt(vi, zr, zi, ALU.add))
                for q in range(2):
                    dve.memset(HP[:, q, :, 0:1], 0.0)
                    dve.tensor_copy(HP[:, q, :, 1:NCH], V[:, q, :, 0:NCH - 1])
                    last = dve.tensor_copy(HP[:, q, :, NCH:NC], h0[:, q, :, :].rearrange("p b i -> p i b"))
                    dve.tensor_copy(s1[:, 20 + q, :], V[:, q, :, NCH - 1])
                step(last)
                dve.sem_inc(sem("ss_HP"), 1)
                p8 = [pw[:, q, L, :].rearrange("p (o i) -> p o i", o=1).broadcast_to((P, DB, GP)) for q in range(2)]
                h0r, h0i = h0[:, 0, :, :], h0[:, 1, :, :]
                u1 = B[:, 0, :, :].rearrange("p i c -> p (i c)")[:, 0:P].rearrange("p (b i) -> p b i", b=DB)
                u2 = B[:, 1, :, :].rearrange("p i c -> p (i c)")[:, 0:P].rearrange("p (b i) -> p b i", b=DB)
                for q, (x0, x1, op) in enumerate(((h0r, h0i, ALU.subtract), (h0i, h0r, ALU.add))):
                    tt(u1, x0, p8[0], ALU.mult)
                    step(tt(u2, x1, p8[1], ALU.mult))
                    step(tt(u1, u1, u2, op))
                    step(tt(tA[:, q * P:(q + 1) * P].rearrange("p (b i) -> p b i", b=DB), u1,
                            V[:, q, :, NCH:NC].rearrange("p i b -> p b i"), ALU.add))
                dve.sem_inc(sem("ss_hs"), 1)
                dve.wait_ge(sem("ss_hps"), 1)
                dve.tensor_copy(hout[0:GP, 0:2, :].rearrange("p n s -> p (n s)"), bank[0][0:GP, 0:2 * P])
                dve.tensor_copy(hout[:, 2:4, :].rearrange("p n s -> p (n s)"), bank[1][:, 0:2 * P])\
                   .then_inc(sem("ss_hout"), 1)

    with ExitStack() as ctx:
        sb = alloc(ctx)
        yT = sb("yT", [P, 4, L * NC])
        wg = sb("wg", [P, 4, DA])
        bg = sb("bg", [P, 4])
        gate = sb("gate", [P, 2, 4, 272])
        sT = sb("sT", [P, 4, TP])
        NQ = L * NC // 4
        with nc.Block() as block:
            @block.sync
            def _(sp):
                for q in range(4):
                    sp.dma_start(yT[:, q, :], scr_y[8 * q:8 * q + 8, :, :, :].rearrange("g c j n -> (g c) (j n)"))\
                      .then_inc(sem("yT_in"), 16)
                sp.dma_start(wg[:, :, :], a["ssm_w_glu"].rearrange("o (k p) n -> p (o k) n", p=P)).then_inc(sem("yT_in"), 16)
                with nc.allow_non_contiguous_dma(reason="2 KB in all"):
                    sp.dma_start(bg[:, :], a["ssm_b_glu"][0].rearrange("(q p) -> p q", p=P)).then_inc(sem("yT_in"), 16)
                sp.wait_ge(sem("gl_s"), 5)
                sp.dma_start(scr_s, sT[:, :, :]).then_inc(sem("s_out"), 16)
                sp.wait_ge(sem("s_out"), 16)

            @block.tensor
            def _(pe):
                pe.wait_ge(sem("yT_in"), 96)
                for b in range(4):
                    for q in range(4):
                        n = 4 * b + q
                        if n >= 8:
                            pe.wait_ge(sem("gl_gate"), n - 7)
                        for k in range(4):
                            last = pe.matmul(bank[n % 8][:, 0:NQ], wg[:, k, q * P:(q + 1) * P],
                                             yT[:, k, b * NQ:(b + 1) * NQ], start=k == 0, stop=k == 3)
                        last.then_inc(sem("gl_ps"), 1)

            @block.scalar
            def _(act):
                for b in range(4):
                    if b >= 2:
                        act.wait_ge(sem("gl_s"), b)
                    for q in range(4):
                        n = 4 * b + q
                        act.wait_ge(sem("gl_ps"), n + 1)
                        act.activation(gate[:, b % 2, q, :], bank[n % 8][:, 0:NQ], ACT.Sigmoid, bias=bg[:, q:q + 1])\
                           .then_inc(sem("gl_gate"), 1)

            @block.vector
            def _(dve):
                dve.memset(sT[:, :, SEQ + SR:TP], 0.0).then_inc(sem("gl_s"), 1)
                for b in range(4):
                    dve.wait_ge(sem("gl_gate"), 4 * b + 4)
                    for q in range(4):
                        last = dve.tensor_tensor(
                            sT[:, q, 0:SEQ + SR].rearrange("p (n j) -> p j n", j=L)[:, 2 * b:2 * b + 2, :],
                            yT[:, q, b * NQ:(b + 1) * NQ].rearrange("p (j n) -> p j n", j=2),
                            gate[:, b % 2, q, :].rearrange("p (j n) -> p j n", j=2), ALU.mult)
                    last.then_inc(sem("gl_s"), 1)


def trunk(nc, a, o, alloc, sem, ident, kT, vrows, neglam, bank, psum, scr_q, scr_s):
    with ExitStack() as ctx:
        sb = alloc(ctx)
        w_out = sb("w_out_sb", [P, KC, DM])
        keysT = sb("keysT", [P, 2 * EH, NKEY])
        wq = sb("wq", [P, 2, KC, 2 * NKEY])
        lng = sb("lng", [P, 4, DM])
        subg = sb("subg", [P, DV])
        gk = sb("gk", [P, 2])
        dist = sb("dist", [P, SEQ])
        bias = sb("bias", [P, SEQ + DS])
        xin = sb("xin", [P, DM])
        qT = sb("qT", [P, H, P])
        sT = sb("sT_t", [P, 4, P])
        oT = sb("oT", [P, 4, P])
        E = sb("E", [P, 2 * SEQ])
        aT = sb("aT", [P, KC, P])
        x1 = sb("x1", [P, DM])
        x1c = sb("x1c", [P, DM])
        junk = sb("junk", [P, 2, DM], mybir.dt.bfloat16)
        y = sb("y", [P, DM])
        Ur = sb("Ur", [P, RING, DM])
        Vr = sb("Vr", [P, RING, DM])
        D = sb("D", [P, RING, P])
        small = sb("small", [P, 64])
        bn = sb("bn", [P, 2, 6])
        mv = sb("mv", [P, 2])
        bn2 = sb("bn2", [P, 2, 6])
        mv2 = sb("mv2", [P, 2])
        qh = sb("qh", [P, 2 * NKEY])
        qTh = sb("qTh", [P, 2, P])
        sc = sb("sc", [P, 2, 2 * NKEY])
        sc2 = sb("sc2", [P, 2 * NKEY])
        cand = sb("cand", [P, TOP * TOP])
        vt = sb("vt", [P, 2 * EH, TOP])
        it = sb("it", [P, 2 * EH, TOP], U32)
        itf = sb("itf", [P, 2 * EH, TOP])
        best = sb("best", [P, EH, TOP])
        pos = sb("pos", [P, EH, TOP], U32)
        pint = sb("pint", [P, NK], U32)
        pf = sb("pf", [P, NK])
        key = sb("key", [P, 2, NK])
        gates = sb("gates", [P, EH, TOP])
        gcur = sb("gcur", [P, NK])
        icur = sb("icur", [P, NK], U32)
        iot_i = sb("iot_i", [P, TOP], I32)
        iot = sb("iot", [P, TOP])
        acts = sb("acts", [P, RING])
        ge = sb("ge", [P, RING])
        qbd = sb("qbd", [P, H, 64])
        vnew = sb("vnew", [DS, DA])
        PTn = sb("PTn", [DS, 64])
        sel = sb("sel", [64, P])
        rowc = sb("rowc", [64, 8])
        headm = sb("headm", [64, H])
        wm = sb("wm", [64, H])
        rowi = sb("rowi", [64, 2], I32)
        pages = sb("pages", [1, DB * PG], I32)
        Kst = wq[:, :, :, :].rearrange("p s k n -> p s (k n)").rearrange("p s (g n) -> p s g n", n=DA)

        Ef = E[:, :]

        def S2(c):
            return psum[:, 2 * c:2 * c + 2, :].rearrange("p b n -> p (b n)")

        y_prompt = o[0].rearrange("b t d -> (b t) d")
        y_sample = o[1].rearrange("b t d -> (b t) d")
        wq_v = a["peer_w_q"][0].rearrange("(k p) n -> p k n", p=P)
        ku = a["cache_k"].rearrange("d g t h c q -> (d g) t (h c q)")
        vu = a["cache_v"].rearrange("d g t h v -> (d g) t (h v)")
        U_tab = a["peer_u"][0]
        V_tab = a["peer_v"][0]

        def wait(eng, name, value, hold=False):
            if isinstance(value, int) and value <= 0:
                return
            eng.wait_ge(sem(name), value)
            if hold and not isinstance(value, int):
                eng.sem_inc(sem("held_" + str(hold)), 1)

        def sp_pages(sp, b, kind, half):
            for pg in range(4 * half, 4 * half + 4):
                page = sp.value_load(pages[0:1, PG * b + pg:PG * b + pg + 1], min_val=0, max_val=ku.shape[0] - 1)
                src, dst, name = (ku, Kst[:, pg // 4, pg % 4, :], f"s_K{half}") if kind == "k" else \
                    (vu, vrows[:, pg, :], "s_V")
                sp.dma_start(dst, src[bass.ds(page, 1), :, :].rearrange("g t n -> (g t) n")).then_inc(sem(name), 16)

        def sp_front(sp, t, rows):
            src = a["x_all"][bass.ds(t * P, P), :]
            if rows == P:
                wait(sp, "scores", 4 * t)
            else:
                wait(sp, "scores", 4 * NT)
            sp.dma_start(qT[:, :, :], scr_q[:, :, bass.ds(t * P, P)]).then_inc(sem("q_in"), 16)
            wait(sp, "h_ready", 2 * t)
            sp.dma_start(sT[:, :, :], scr_s[:, :, bass.ds(t * P, P)]).then_inc(sem("sT_in"), 16)
            wait(sp, "x1_ready", t)
            sp.dma_start(xin[:, :], src).then_inc(sem("xin"), 16)
            if rows != P:
                wait(sp, "q_ps", EH * NT)
                sp_pages(sp, 0, "k", 0)
                sp_pages(sp, 0, "k", 1)
                for b in range(DB):
                    wait(sp, "s_O", b)
                    sp_pages(sp, b, "v", 0)
                    sp_pages(sp, b, "v", 1)
                    sp.dma_start(vnew[:, :], vrows[DS * b:DS * b + DS, NT, :]).then_inc(sem("vnew_in"), 16)
                    if b < DB - 1:
                        for half in range(2):
                            wait(sp, "s_KTps", 8 * b + 4 * half + 4)
                            sp_pages(sp, b + 1, "k", half)
                wait(sp, "s_KTps", 8 * DB)
            for e in range(EH):
                wait(sp, "q_ps", 8 * t + e - 1)
                sp.dma_start(wq[:, e % 2, :, :], wq_v[:, :, 2 * NKEY * e:2 * NKEY * (e + 1)])\
                  .then_inc(sem(f"wq_in{e % 2}"), 16)

        def pool_gather(pool, t, k, rows, tab, ring, free, arrived):
            wait(pool, free, NK * t + k + 1, hold="pool")
            pool.indirect_dma_start(out=ring[:rows, k % RING, :], out_offset=None, in_=tab,
                                    in_offset=bass.IndirectOffsetOnAxis(ap=icur[:rows, k:k + 1], axis=0))\
                .then_inc(sem(f"{arrived}{k % RING}"), 16)

        def pool_expert(pool, t, k, rows):
            if k == 0:
                wait(pool, "cur_ready", t + 1, hold="pool")
            if k < NK:
                pool_gather(pool, t, k, rows, U_tab, Ur, "dot_done", "u_in")
            if k >= 2:
                pool_gather(pool, t, k - 2, rows, V_tab, Vr, "vsum_done", "v_in")

        def pe_scores(pe, t, h):
            wait(pe, "q_in", 16 * t + 16)
            if h == 0:
                wait(pe, "sc_ready", EH * t)
            wait(pe, "aT_ready", 4 * t + h, hold="pe")
            for c in range(2):
                for e in range(2):
                    last = pe.matmul(bank[2 * c + e][:, :], qT[64 * c:64 * c + 64, h, :],
                                     kT[64 * c:64 * c + 64, h, 512 * e:512 * e + 512], start=True, stop=True)
            last.then_inc(sem("scores"), 1)

        def pe_map_columns(pe, t, h):
            wait(pe, "map_ready", 4 * t + h + 1, hold="pe")
            for j in range(NT):
                last = pe.transpose(bank[j // 4][:, j % 4 * P:(j % 4 + 1) * P], Ef[:, SEQ + j * P:SEQ + (j + 1) * P], ident[:, :])
            last.then_inc(sem("aT_ps"), 1)

        def pe_values(pe, t, h):
            wait(pe, "aT_ready", 4 * t + h + 1, hold="pe")
            for j in range(NT):
                last = pe.matmul(bank[4][:, h * DV:(h + 1) * DV], aT[:, j, :], vrows[:, j, h * DV:(h + 1) * DV],
                                 start=j == 0, stop=j == NT - 1)
            last.then_inc(sem("o_ready"), 1)

        def pe_sample_keys(pe, b, r):
            for pg in (2 * r, 2 * r + 1):
                if pg % 4 == 0:
                    wait(pe, f"s_K{pg // 4}", 64 * (b + 1))
                wait(pe, "s_KT", 8 * b + pg - 1)
                for h in range(H):
                    last = pe.transpose(bank[(3, 5)[pg % 2]][:, h * P:(h + 1) * P],
                                        Kst[:, pg // 4, pg % 4, h * P:(h + 1) * P], ident[:, :])
                last.then_inc(sem("s_KTps"), 1)

        def pe_sample_scores(pe, b, half):
            if half == 0:
                wait(pe, "q_in", 16 * NT + 16)
                wait(pe, "s_KT", 8 * b + 8)
                wait(pe, "s_qbd", b + 1)
                wait(pe, "s_Om", b)
            for e, (k0, n) in list(enumerate(((0, 512), (512, 512), (SEQ + DS * b, DS))))[half:2 * half + 1]:
                for h in range(H):
                    last = pe.matmul(bank[e][0:64, 0:n], qbd[:, h, :], kT[:, h, k0:k0 + n], start=h == 0, stop=h == H - 1)
            if half:
                last.then_inc(sem("s_scores"), 1)

        def pe_sample_map(pe, b):
            wait(pe, "s_exp", b + 1)
            for pg in range(PG):
                pe.transpose(bank[0][:, 64 * pg:64 * pg + 64], Ef[0:64, P * pg:P * pg + P], ident[0:64, 0:64])
            pe.transpose(bank[1][0:DS, 0:64], Ef[0:64, SEQ:SEQ + DS], ident[0:64, 0:64]).then_inc(sem("s_PTps"), 1)

        def pe_sample_values(pe, b):
            wait(pe, "s_PT", b + 1)
            wait(pe, "s_V", 128 * (b + 1))
            wait(pe, "vnew_in", 16 * (b + 1))
            for pg in range(PG):
                pe.matmul(bank[2][0:64, :], aT[:, pg, 0:64], vrows[:, pg, :], start=pg == 0, stop=False)
            pe.matmul(bank[2][0:64, :], PTn[:, :], vnew[:, :], start=False, stop=True).then_inc(sem("s_O"), 1)

        def pe_sample_sum(pe, b):
            wait(pe, "s_Om", b + 1)
            pe.matmul(bank[4][0:64, :], sel[:, 56 - DS * b:120 - DS * b], Ef[0:64, SEQ + 16:SEQ + 16 + DA],
                      start=b == 0, stop=b == DB - 1).then_inc(sem("s_acc"), 1)

        def pe_output(pe, t, r, rows):
            if r == 3:
                wait(pe, "on_ready", t + 1, hold="pe")
                for h in range(H):
                    last = pe.transpose(bank[5][:, h * P:h * P + rows], Ef[:rows, h * P:(h + 1) * P], ident[:rows, :rows])
                last.then_inc(sem("oT_ps"), 1)
            if r in (5, 6):
                wait(pe, "oT_ready", t + 1)
                wait(pe, "sT_in", 16 * t + 16, hold="pe")
                e = r - 5
                for k in range(KC):
                    cols = (oT if k < 4 else sT)[:, k % 4, :rows]
                    last = pe.matmul(bank[e][:rows, :], cols, w_out[:, k, 512 * e:512 * e + 512],
                                     start=k == 0, stop=k == KC - 1)
                last.then_inc(sem("h_ready"), 1)
            if r == 13:
                wait(pe, "x1_ready", t + 1, hold="pe")
                for k in range(KC):
                    last = pe.transpose(bank[2 + k // 4][:, k % 4 * P:k % 4 * P + rows], x1[:rows, k * P:(k + 1) * P],
                                        ident[:rows, :rows])
                last.then_inc(sem("x1T_ps"), 1)

        def pe_head(pe, t, e, r, rows):
            n = EH * t + e
            if r == 0:
                if e == 0:
                    wait(pe, "x1T_ready", t + 1)
                wait(pe, f"wq_in{e % 2}", 64 * t + 16 * (e // 2) + 16)
                wait(pe, "q_copied", n, hold="pe")
                for k in range(KC):
                    last = pe.matmul(bank[4][:rows, 0:2 * NKEY], aT[:, k, :rows], wq[:, e % 2, k, :], start=k == 0, stop=k == KC - 1)
                last.then_inc(sem("q_ps"), 1)
            if r == 2:
                wait(pe, "q_copied", n + 1, hold="pe")
                for c in range(2):
                    last = pe.transpose(bank[5][:, c * P:c * P + rows], qh[:rows, c * NKEY:(c + 1) * NKEY], ident[:rows, :rows])
                last.then_inc(sem("qT_ps"), 1)
            if r == 4:
                wait(pe, "sc_ready", n)
                wait(pe, "qT_ready", n + 1, hold="pe")
                for c in range(2):
                    last = pe.matmul(bank[0][:rows, c * NKEY:(c + 1) * NKEY], qTh[:, c, :rows], keysT[:, 2 * e + c, :],
                                     start=True, stop=True)
                last.then_inc(sem("sc_ps"), 1)

        def pe_front(pe, t, k, rows):
            if rows == P:
                h, r = divmod(k, AT)
                if h < H:
                    if r == 0:
                        pe_scores(pe, t, h)
                    if r == 8:
                        pe_map_columns(pe, t, h)
                    if r == 10:
                        pe_values(pe, t, h)
            else:
                b, r = divmod(k, 8)
                if 1 <= b <= DB and r == 0:
                    pe_sample_values(pe, b - 1)
                if 1 <= b <= DB and r == 2:
                    pe_sample_sum(pe, b - 1)
                if b < DB:
                    if r < 4:
                        pe_sample_keys(pe, b, r)
                    if r in (4, 5):
                        pe_sample_scores(pe, b, r - 4)
                    if r == 7:
                        pe_sample_map(pe, b)
            pe_output(pe, t, k - base(rows), rows)
            for e, r in heads_at(k, rows):
                pe_head(pe, t, e, r, rows)

        def pe_expert(pe, t, k, rows):
            if k == 0:
                wait(pe, "sum_read", t + 1)
            wait(pe, f"v_in{k % RING}", 16 * (NK // RING * t + k // RING + 1))
            wait(pe, "diag_done", NK * t + k + 1, hold="pe")
            for e in range(2):
                ins = pe.matmul(bank[6 + e][:rows, :], D[:rows, k % RING, :rows], Vr[:rows, k % RING, 512 * e:512 * e + 512],
                                start=k == 0, stop=k == NK - 1)
            ins.then_inc(sem("vsum_done"), 1)

        def act_attention(act, t, h, r):
            if r == 4:
                wait(act, "max_ready", 4 * t + h + 1)
                for c in range(2):
                    last = act.activation(Ef[:, c * SEQ:(c + 1) * SEQ], Ef[:, c * SEQ:(c + 1) * SEQ], ACT.Exp,
                                          bias=small[:, 2 + c:3 + c], accum_out=small[:, 4 + c:5 + c])
                last.then_inc(sem("exp_ready"), 1)
            if r == 9:
                wait(act, "aT_ps", 4 * t + h + 1)
                for e in range(2):
                    last = act.activation(aT[:, 4 * e:4 * e + 4, :].rearrange("p k t -> p (k t)"), bank[e][:, :], ACT.Copy)
                last.then_inc(sem("aT_ready"), 1)

        def act_sample(act, b, r):
            if r < 4:
                for pg in (2 * r, 2 * r + 1):
                    if pg == 0:
                        wait(act, "s_scores", b)
                    wait(act, "s_KTps", 8 * b + pg + 1)
                    act.activation(kT[:, :, pg * P:(pg + 1) * P], bank[(3, 5)[pg % 2]][:, :].rearrange("p (h t) -> p h t", h=H),
                                   ACT.Copy).then_inc(sem("s_KT"), 1)
            if r == 6:
                wait(act, "s_max", b + 1)
                act.activation(Ef[0:64, 0:SEQ + DS], Ef[0:64, 0:SEQ + DS], ACT.Exp, bias=small[0:64, 2:3],
                               accum_out=small[0:64, 4:5]).then_inc(sem("s_exp"), 1)
            if r == 7:
                wait(act, "s_PTps", b + 1)
                act.activation(aT[:, :, 0:64], bank[0][:, :].rearrange("p (g r) -> p g r", g=PG), ACT.Copy)
                act.activation(PTn[:, :], bank[1][0:DS, 0:64], ACT.Copy).then_inc(sem("s_PT"), 1)

        def act_output(act, t, r, rows):
            if r == 1:
                wait(act, "ss_ready", t + 1)
                act.activation(small[:rows, 12:16], small[:rows, 8:12], ACT.Sqrt).then_inc(sem("sr_ready"), 1)
            if r == 10:
                wait(act, "var_ready", t + 1)
                act.activation(small[:rows, 17:18], small[:rows, 16:17], ACT.Sqrt).then_inc(sem("sd_ready"), 1)
            if r == 14:
                wait(act, "x1T_ps", t + 1)
                for e in range(2):
                    last = act.activation(aT[:, 4 * e:4 * e + 4, :rows],
                                          bank[2 + e][:, :].rearrange("p (k t) -> p k t", k=4)[:, :, :rows], ACT.Copy)
                last.then_inc(sem("x1T_ready"), 1)

        def act_head(act, t, e, r, rows):
            n = EH * t + e
            if r == 1:
                wait(act, "q_ps", n + 1)
                act.activation(qh[:rows, :], bank[4][:rows, 0:2 * NKEY], ACT.Square, accum_out=small[:rows, 24 + e:25 + e])\
                   .then_inc(sem("q_sq"), 1)
                wait(act, "q_sq", n + 1)
                act.activation(qh[:rows, :], bank[4][:rows, 0:2 * NKEY], ACT.Copy).then_inc(sem("q_copied"), 1)
            if r == 3:
                wait(act, "qT_ps", n + 1)
                act.activation(qTh[:, :, :rows], bank[5][:, 0:2 * P].rearrange("p (c t) -> p c t", c=2)[:, :, :rows], ACT.Copy)\
                   .then_inc(sem("qT_ready"), 1)
            if r == 5:
                wait(act, "sc_ps", n + 1)
                wait(act, "topk_done", n - 1)
                act.activation(sc[:rows, e % 2, :], bank[0][:rows, 0:2 * NKEY], ACT.Copy).then_inc(sem("sc_ready"), 1)

        def act_combine(act, t, r, rows):
            if r == 1:
                wait(act, "qs_ready", t + 1)
                act.activation(small[:rows, 40:48], small[:rows, 32:40], ACT.Sqrt).then_inc(sem("qr_ready"), 1)
            if r == 3:
                wait(act, "lg_ready", t + 1)
                act.activation(gates[:rows, :, :], best[:rows, :, :], ACT.Exp).then_inc(sem("ex_ready"), 1)

        def act_front(act, t, k, rows):
            if rows == P:
                h, r = divmod(k, AT)
                if h < H:
                    act_attention(act, t, h, r)
            else:
                b, r = divmod(k, 8)
                if b < DB:
                    act_sample(act, b, r)
            act_output(act, t, k - base(rows), rows)
            for e, r in heads_at(k, rows):
                act_head(act, t, e, r, rows)
            act_combine(act, t, k - combine_at(rows), rows)

        def act_expert(act, t, k, rows):
            wait(act, "dot_done", NK * t + k + 1 + RING)
            j = k % RING
            act.activation(ge[:rows, j:j + 1], acts[:rows, j:j + 1], ACT.Gelu).then_inc(sem("gelu_done"), 1)

        def act_finish(act, t, rows):
            wait(act, "var2_ready", t + 1)
            act.activation(small[:rows, 19:20], small[:rows, 18:19], ACT.Sqrt).then_inc(sem("sd2_ready"), 1)
            wait(act, "y_ready", t + 1)
            dst = y_prompt[bass.ds(t * P, P), :] if rows == P else y_sample
            act.dma_start(dst, y[:rows, :]).then_inc(sem("y_out3"), 16)

        def dve_attention(dve, step, t, h, r):
            if h == 0 and r == 0:
                if not (isinstance(t, int) and t == 0):
                    step(dve.tensor_scalar(dist[:, :], dist[:, :], -float(P), None, ALU.add))
                step(dve.tensor_scalar(bias[:, 0:SEQ], dist[:, :], 0.0, MASKED, ALU.is_gt, ALU.mult))
                step(dve.tensor_tensor(bias[:, 0:SEQ], bias[:, 0:SEQ], dist[:, :], ALU.add))
            if r in (2, 3):
                c = r - 2
                wait(dve, "aT_ps", 4 * t + h)
                wait(dve, "scores", 4 * t + h + 1, hold="dve")
                step(dve.tensor_tensor_reduce(out=Ef[:, c * SEQ:(c + 1) * SEQ], in0=S2(c), in1=bias[:, 0:SEQ],
                                              scale=SLOPE[h], scalar=LOW, op0=ALU.add, op1=ALU.max,
                                              accum_out=small[:, c:c + 1]))
                if c:
                    dve.tensor_scalar(small[:, 2:4], small[:, 0:2], -1.0, None, ALU.mult).then_inc(sem("max_ready"), 1)
            if r == 6:
                wait(dve, "exp_ready", 4 * t + h + 1)
                step(dve.reciprocal(small[:, 6:8], small[:, 4:6]))
                step(dve.tensor_scalar(small[:, 7:8], small[:, 7:8], neglam[:, 0:1], None, ALU.mult))
                step(dve.tensor_scalar(Ef[:, 0:SEQ], Ef[:, 0:SEQ], small[:, 6:7], None, ALU.mult))
            if r == 7:
                dve.scalar_tensor_tensor(out=Ef[:, SEQ:], in0=Ef[:, SEQ:], scalar=small[:, 7:8], in1=Ef[:, 0:SEQ],
                                         op0=ALU.mult, op1=ALU.add).then_inc(sem("map_ready"), 1)

        def dve_sample_setup(dve, step):
            wait(dve, "aT_ps", 4 * NT)
            step(dve.tensor_scalar(bias[0:64, 0:SEQ], dist[0:64, :], rowc[:, 6:7], None, ALU.add))
            step(dve.tensor_scalar(bias[0:64, SEQ:], iot[0:64, 0:DS], rowc[:, 0:1], None, ALU.subtract))
            step(dve.tensor_scalar(Ef[0:64, 0:SEQ + DS], bias[0:64, :], 0.0, MASKED, ALU.is_gt, ALU.mult))
            step(dve.tensor_tensor(bias[0:64, :], bias[0:64, :], Ef[0:64, 0:SEQ + DS], ALU.add))

        def dve_sample(dve, step, b, r):
            if r == 0:
                wait(dve, "q_in", 16 * NT + 16)
                wait(dve, "s_scores", b)
                flat = qbd[:, :, :].rearrange("p h r -> p (h r)")
                for c in range(2):
                    for h in range(H):
                        last = dve.tensor_copy(flat[64 * c:64 * c + 64, 80 * h + DS * c:80 * h + DS * c + DS],
                                               qT[64 * c:64 * c + 64, h, DS * b:DS * b + DS])
                last.then_inc(sem("s_qbd"), 1)
            if r == 5:
                wait(dve, "s_acc", b)
                wait(dve, "s_scores", b + 1)
                S = psum[0:64, 0:3, :].rearrange("p b n -> p (b n)")[:, 0:SEQ + DS]
                step(dve.tensor_tensor(Ef[0:64, 0:SEQ + DS], S, bias[0:64, :], ALU.add))
                step(dve.tensor_scalar(Ef[0:64, 0:SEQ + DS], Ef[0:64, 0:SEQ + DS], rowc[:, 1:2], None, ALU.mult))
            if r == 6:
                step(dve.reduce_max(small[0:64, 0:1], Ef[0:64, 0:SEQ + DS], X))
                dve.tensor_scalar(small[0:64, 2:3], small[0:64, 0:1], -1.0, None, ALU.mult).then_inc(sem("s_max"), 1)
            if r == 7:
                wait(dve, "s_exp", b + 1)
                step(dve.reciprocal(small[0:64, 6:7], small[0:64, 4:5]))
                step(dve.tensor_scalar(small[0:64, 6:7], small[0:64, 6:7], rowc[:, 2:3], None, ALU.mult))
                step(dve.tensor_scalar(wm[:, :], headm[:, :], small[0:64, 6:7], None, ALU.mult))

        def dve_sample_rows(dve, b):
            wait(dve, "s_O", b + 1)
            dve.tensor_tensor(Ef[0:64, SEQ + 16:SEQ + 16 + DA].rearrange("p (h v) -> p h v", h=H),
                              bank[2][0:64, :].rearrange("p (h v) -> p h v", h=H),
                              wm[:, :].rearrange("p (h u) -> p h u", u=1).broadcast_to((64, H, DV)), ALU.mult)\
               .then_inc(sem("s_Om"), 1)

        def layer_norm(dve, step, x, rows, gain, stats, agg, col, var_sem, sd_sem, n, part):
            if part == 0:
                for e in range(2):
                    ins = dve.bn_stats(stats[:rows, e, :], x[:rows, 512 * e:512 * e + 512])
                step(ins)
                step(dve.bn_aggr(agg[:rows, :], stats[:rows, :, :].rearrange("p a b -> p (a b)")))
                dve.tensor_scalar(small[:rows, col:col + 1], agg[:rows, 1:2], EPS, None, ALU.add).then_inc(sem(var_sem), 1)
            if part == 1:
                wait(dve, sd_sem, n)
                step(dve.reciprocal(small[:rows, col + 1:col + 2], small[:rows, col + 1:col + 2]))
                step(dve.tensor_scalar(x[:rows, :], x[:rows, :], agg[:rows, 0:1], small[:rows, col + 1:col + 2],
                                       ALU.subtract, ALU.mult))
                step(dve.tensor_tensor(x[:rows, :], x[:rows, :], lng[:rows, gain, :], ALU.mult))
            if part == 2:
                return dve.tensor_tensor(x[:rows, :], x[:rows, :], lng[:rows, gain + 1, :], ALU.add)

        def dve_output(dve, step, t, r, rows):
            if r == 0:
                if rows == P:
                    wait(dve, "o_ready", 4 * t + 4)
                else:
                    wait(dve, "s_acc", DB)
                step(dve.tensor_copy(Ef[:rows, 0:DA], bank[4][:rows, :]))
                step(dve.tensor_tensor(Ef[:rows, DA:2 * DA], Ef[:rows, 0:DA], Ef[:rows, 0:DA], ALU.mult))
                step(dve.reduce_sum(small[:rows, 8:12], Ef[:rows, DA:2 * DA].rearrange("p (h v) -> p h v", h=H), X))
                dve.tensor_scalar(small[:rows, 8:12], small[:rows, 8:12], 1.0 / DV, EPS, ALU.mult, ALU.add)\
                   .then_inc(sem("ss_ready"), 1)
            if r == 2:
                wait(dve, "sr_ready", t + 1)
                step(dve.reciprocal(small[:rows, 12:16], small[:rows, 12:16]))
                for h in range(H):
                    ins = dve.scalar_tensor_tensor(out=Ef[:rows, h * DV:(h + 1) * DV], in0=Ef[:rows, h * DV:(h + 1) * DV],
                                                   scalar=small[:rows, 12 + h:13 + h], in1=subg[:rows, :],
                                                   op0=ALU.mult, op1=ALU.mult)
                ins.then_inc(sem("on_ready"), 1)
            if r == 4:
                wait(dve, "oT_ps", t + 1)
                dve.tensor_copy(oT[:, :, :rows], bank[5][:, :].rearrange("p (h t) -> p h t", h=H)[:, :, :rows])\
                   .then_inc(sem("oT_ready"), 1)
            if r == 9:
                wait(dve, "xin", 16 * t + 16)
                wait(dve, "h_ready", 2 * t + 2)
                for e in range(2):
                    ins = dve.scalar_tensor_tensor(out=x1[:rows, 512 * e:512 * e + 512], in0=xin[:rows, 512 * e:512 * e + 512],
                                                   scalar=ALPHA, in1=bank[e][:rows, :], op0=ALU.mult, op1=ALU.add)
                step(ins)
            if r in (10, 11, 12):
                ins = layer_norm(dve, step, x1, rows, 0, bn, mv, 16, "var_ready", "sd_ready", t + 1, r - 10)
                if r == 12:
                    ins.then_inc(sem("x1_ready"), 1)

        def dve_topk(dve, step, src, scratch, vals, idxs):
            step(dve.max(vals[:, 0:8], src))
            step(dve.max_index(idxs[:, 0:8], vals[:, 0:8], src))
            step(dve.match_replace(scratch, vals[:, 0:8], src, LOW))
            step(dve.max(vals[:, 8:16], scratch))
            step(dve.max_index(idxs[:, 8:16], vals[:, 8:16], scratch))

        def dve_head(dve, step, t, e, r, rows):
            if r in (6, 7):
                c = r - 6
                wait(dve, "sc_ready", EH * t + e + 1, hold="dve")
                dve_topk(dve, step, sc[:rows, e % 2, c * NKEY:(c + 1) * NKEY], sc2[:rows, 0:NKEY],
                         vt[:rows, 2 * e + c, :], it[:rows, 2 * e + c, :])
                if c:
                    dve.sem_inc(sem("topk_done"), 1)
            if r == 8:
                cv = cand[:rows, :].rearrange("p (i j) -> p i j", i=TOP)
                step(dve.tensor_tensor(cv, vt[:rows, 2 * e, :].rearrange("p (i u) -> p i u", u=1).broadcast_to((rows, TOP, TOP)),
                                       vt[:rows, 2 * e + 1, :].rearrange("p (u j) -> p u j", u=1).broadcast_to((rows, TOP, TOP)),
                                       ALU.add))
            if r == 9:
                dve_topk(dve, step, cand[:rows, :], sc2[:rows, :], best[:rows, e, :], pos[:rows, e, :])

        def dve_combine(dve, step, t, r, rows):
            eq = Ef[:rows, 0:NK * TOP].rearrange("p (e k i) -> p e k i", e=EH, k=TOP)
            if r == 0:
                wait(dve, "q_copied", EH * t + EH)
                dve.tensor_scalar(small[:rows, 32:40], small[:rows, 24:32], 1.0 / (2 * NKEY), EPS, ALU.mult, ALU.add)\
                   .then_inc(sem("qs_ready"), 1)
                step(dve.tensor_copy(itf[:rows, :, :], it[:rows, :, :]))
            if r == 2:
                wait(dve, "qr_ready", t + 1)
                step(dve.reciprocal(small[:rows, 40:48], small[:rows, 40:48]))
                step(dve.tensor_copy(small[:rows, 48:56], best[:rows, :, 0]))
                step(dve.tensor_tensor(best[:rows, :, :], best[:rows, :, :],
                                       small[:rows, 48:56].rearrange("p (e u) -> p e u", u=1).broadcast_to((rows, EH, TOP)), ALU.subtract))
                dve.tensor_tensor(best[:rows, :, :], best[:rows, :, :],
                                  small[:rows, 40:48].rearrange("p (e u) -> p e u", u=1).broadcast_to((rows, EH, TOP)), ALU.mult)\
                   .then_inc(sem("lg_ready"), 1)
            for c, (op, n) in enumerate(((ALU.logical_shift_right, 4), (ALU.bitwise_and, 15))):
                if r == 3 + 3 * c:
                    step(dve.tensor_scalar(pint[:rows, :], pos[:rows, :, :].rearrange("p e k -> p (e k)"), n, None, op))
                    step(dve.tensor_copy(pf[:rows, :], pint[:rows, :]))
                    step(dve.tensor_tensor(eq, pf[:rows, :].rearrange("p (e k u) -> p e k u", e=EH, u=1).broadcast_to((rows, EH, TOP, TOP)),
                                           iot[:rows, :].rearrange("p (a b i) -> p a b i", a=1, b=1).broadcast_to((rows, EH, TOP, TOP)),
                                           ALU.is_equal))
                if r == 4 + 3 * c:
                    keys = itf[:rows, :, :].rearrange("p (e c) i -> p e c i", c=2)[:, :, c:c + 1, :].broadcast_to((rows, EH, TOP, TOP))
                    step(dve.tensor_tensor(eq, eq, keys, ALU.mult))
                if r == 5 + 3 * c:
                    step(dve.reduce_sum(key[:rows, c, :], eq, X))
            if r == 9:
                step(dve.scalar_tensor_tensor(out=key[:rows, 0, :], in0=key[:rows, 0, :], scalar=float(NKEY), in1=key[:rows, 1, :],
                                              op0=ALU.mult, op1=ALU.add))
                wait(dve, "ex_ready", t + 1)
                step(dve.reduce_sum(small[:rows, 48:56], gates[:rows, :, :], X))
                step(dve.reciprocal(small[:rows, 48:56], small[:rows, 48:56]))
                step(dve.tensor_tensor(gates[:rows, :, :], gates[:rows, :, :],
                                       small[:rows, 48:56].rearrange("p (e u) -> p e u", u=1).broadcast_to((rows, EH, TOP)), ALU.mult))

        def dve_front(dve, step, t, k, rows):
            if rows == P:
                h, r = divmod(k, AT)
                if h < H:
                    dve_attention(dve, step, t, h, r)
            else:
                b, r = divmod(k, 8)
                if k == 0:
                    dve_sample_setup(dve, step)
                if 1 <= b <= DB and r == 1:
                    dve_sample_rows(dve, b - 1)
                if b < DB:
                    dve_sample(dve, step, b, r)
            dve_output(dve, step, t, k - base(rows), rows)
            for e, r in heads_at(k, rows):
                dve_head(dve, step, t, e, r, rows)
            dve_combine(dve, step, t, k - combine_at(rows), rows)

        def dve_diagonal(dve, t, k, rows):
            j = k % RING
            wait(dve, "gelu_done", NK * t + k + 1)
            wait(dve, "vsum_done", NK * t + k + 1)
            dve.tensor_scalar(D[:rows, j, :rows], ident[:rows, :rows], ge[:rows, j:j + 1], gcur[:rows, k:k + 1],
                              ALU.mult, ALU.mult).then_inc(sem("diag_done"), 1)

        def dve_expert(dve, t, k, rows):
            j = k % RING
            wait(dve, f"u_in{j}", 16 * (NK // RING * t + k // RING + 1))
            wait(dve, "dot_done", NK * t + k + RING - 1, hold="dve")
            dve.tensor_tensor_reduce(out=junk[:rows, k % 2, :], in0=Ur[:rows, j, :], in1=x1c[:rows, :], scale=1.0,
                                     scalar=0.0, op0=ALU.mult, op1=ALU.add, accum_out=acts[:rows, j:j + 1])\
               .then_inc(sem("dot_done"), 1)

        def dve_indices(dve, step, t, rows):
            if not (isinstance(t, int) and t == 0):
                wait(dve, f"v_in{RING - 1}", 16 * NK // RING * t)
            step(dve.tensor_copy(icur[:rows, :], key[:rows, 0, :]))
            dve.sem_inc(sem("cur_ready"), 1)

        def dve_sum(dve, step, t, rows):
            wait(dve, "y_out3", 16 * t + 16)
            wait(dve, "vsum_done", NK * t + NK + RING)
            for e in range(2):
                ins = dve.scalar_tensor_tensor(out=y[:rows, 512 * e:512 * e + 512], in0=x1c[:rows, 512 * e:512 * e + 512],
                                               scalar=ALPHA, in1=bank[6 + e][:rows, :], op0=ALU.mult, op1=ALU.add)
            step(ins)
            dve.sem_inc(sem("sum_read"), 1)

        def dve_begin(dve, step, rows):
            dve.tensor_copy(gcur[:rows, :], gates[:rows, :, :].rearrange("p e k -> p (e k)"))
            step(dve.tensor_copy(x1c[:rows, :], x1[:rows, :]))

        def dve_finish(dve, step, t, rows):
            for part in range(3):
                ins = layer_norm(dve, step, y, rows, 2, bn2, mv2, 18, "var2_ready", "sd2_ready", t + 1, part)
            ins.then_inc(sem("y_ready"), 1)

        AT = 12

        def base(rows):
            return 4 * AT if rows == P else 8 * DB + 4

        def spacing(rows):
            return 6 if rows == P else 5

        def heads_at(k, rows):
            start = base(rows) + 15
            return [(e, k - start - spacing(rows) * e) for e in range(EH) if 0 <= k - start - spacing(rows) * e < 10]

        def combine_at(rows):
            return base(rows) + 15 + spacing(rows) * (EH - 1) + 10

        def front_end(rows):
            return combine_at(rows) + 10

        with nc.Block() as block:

            @block.sync
            def _(sp):
                sp.dma_start(pages[:, :], a["page_table"].rearrange("(o b) g -> o (b g)", o=1)).then_inc(sem("pages_in"), 16)
                sp.wait_ge(sem("pages_in"), 16)
                sp.dma_start(Ef.rearrange("p (n d) -> p n d", n=2 * EH), a["peer_sub_keys"][0].rearrange("e c n d -> n (e c) d"))\
                  .then_inc(sem("keys_in"), 16)
                with nc.allow_non_contiguous_dma(reason="1 KB in all"):
                    sp.dma_start(gk[:, :], a["peer_q_g"][0].rearrange("(c d) -> d c", c=2)).then_inc(sem("keys_in"), 16)
                sp.dma_start(subg[:, :], a["attn_subln_g"][0, :].partition_broadcast(P)).then_inc(sem("keys_in"), 16)
                sp.dma_start(w_out[:, :, :], a["w_out"][0].rearrange("(k p) n -> p k n", p=P)).then_inc(sem("w_out_in"), 16)
                for n, name in enumerate(("ln1_g", "ln1_b", "ln2_g", "ln2_b")):
                    sp.dma_start(lng[:, n, :], a[name][0, :].partition_broadcast(P)).then_inc(sem("ln_in"), 16)
                sp_front(sp, 0, P)
                with sp.Fori(0, NT - 1) as t:
                    sp_front(sp, t + 1, P)
                sp_front(sp, NT, SR)
                sp.wait_ge(sem("y_out3"), 16 * (NT + 2))

            @block.gpsimd
            def _(pool):
                pool.iota(dist[:, :].bitcast(I32), [[1, SEQ]], base=0, channel_multiplier=-1).then_inc(sem("iota"), 1)
                pool.iota(iot_i[:, :], [[1, TOP]], base=0, channel_multiplier=0).then_inc(sem("iota"), 1)
                pool.iota(rowi[:, :], [[0, 2]], base=0, channel_multiplier=1).then_inc(sem("iota"), 1)
                pool.memset(qbd[:, :, :], 0.0).then_inc(sem("iota"), 1)
                pool.sem_inc(sem("dot_done"), RING)
                pool.sem_inc(sem("vsum_done"), RING)

                with pool.Fori(0, NT) as t:
                    for k in range(NK + 2):
                        pool_expert(pool, t, k, P)
                for k in range(NK + 2):
                    pool_expert(pool, NT, k, SR)

            @block.tensor
            def _(pe):
                pe.wait_ge(sem("keys_in"), 48)
                for n in range(2 * EH):
                    last = pe.transpose(bank[n // 4][:, n % 4 * P:(n % 4 + 1) * P], Ef[:, n * P:(n + 1) * P], ident[:, :])
                last.then_inc(sem("keys_ps"), 1)
                pe.wait_ge(sem("keys_ready"), 1)
                pe.wait_ge(sem("w_out_in"), 16)

                for k in range(front_end(P)):
                    pe_front(pe, 0, k, P)
                with pe.Fori(0, NT - 1) as t:
                    for k in range(NK):
                        pe_front(pe, t + 1, k, P)
                        pe_expert(pe, t, k, P)
                for k in range(NK):
                    pe_front(pe, NT, k, SR)
                    pe_expert(pe, NT - 1, k, P)
                for k in range(NK, front_end(SR)):
                    pe_front(pe, NT, k, SR)
                for k in range(NK):
                    pe_expert(pe, NT, k, SR)

            @block.scalar
            def _(act):
                for k in range(front_end(P)):
                    act_front(act, 0, k, P)
                with act.Fori(0, NT - 1) as t:
                    for k in range(NK):
                        act_expert(act, t, k, P)
                        act_front(act, t + 1, k, P)
                    act_finish(act, t, P)
                for k in range(NK):
                    act_expert(act, NT - 1, k, P)
                    act_front(act, NT, k, SR)
                for k in range(NK, front_end(SR)):
                    act_front(act, NT, k, SR)
                act_finish(act, NT - 1, P)
                for k in range(NK):
                    act_expert(act, NT, k, SR)
                act_finish(act, NT, SR)

            @block.vector
            def _(dve):
                step = Steps(dve, sem("dve_step3"))
                dve.wait_ge(sem("keys_in"), 48)
                dve.wait_ge(sem("iota"), 4)
                step(dve.tensor_copy(bias[:, 0:SEQ], dist[:, :].bitcast(I32)))
                step(dve.tensor_copy(dist[:, :], bias[:, 0:SEQ]))
                step(dve.tensor_copy(iot[:, :], iot_i[:, :]))
                step(dve.tensor_scalar(subg[:, :], subg[:, :], 1.0 - LAM_INIT, None, ALU.mult))
                dve.wait_ge(sem("keys_ps"), 1)
                for n in range(2 * EH):
                    ins = dve.tensor_scalar(keysT[:, n, :], bank[n // 4][:, n % 4 * P:(n % 4 + 1) * P],
                                            gk[:, n % 2:n % 2 + 1], None, ALU.mult)
                step(ins)
                dve.sem_inc(sem("keys_ready"), 1)
                q, slope, mw, hf, cf, rf = (rowc[:, n:n + 1] for n in range(6))
                step(dve.tensor_copy(rf, rowi[:, 0:1]))
                for dst, sh, mask in ((q, 0, DS - 1), (cf, 3, 1), (hf, 4, H - 1)):
                    step(dve.tensor_scalar(rowi[:, 1:2], rowi[:, 0:1], sh, mask, ALU.arith_shift_right, ALU.bitwise_and))
                    step(dve.tensor_copy(dst, rowi[:, 1:2]))
                step(dve.tensor_tensor(rowc[:, 6:7], rf, q, ALU.subtract))
                step(dve.tensor_scalar(rowc[:, 6:7], rowc[:, 6:7], float(SEQ - P - PAST), None, ALU.add))
                step(dve.tensor_scalar(mw, neglam[0:64, :], -1.0, None, ALU.add))
                step(dve.tensor_scalar(mw, mw, cf, 1.0, ALU.mult, ALU.add))
                step(dve.tensor_scalar(headm[:, :], iot[0:64, 0:H], hf, None, ALU.is_equal))
                step(dve.tensor_scalar(slope, headm[:, 0:1], SLOPE[0], None, ALU.mult))
                for h in range(1, H):
                    step(dve.scalar_tensor_tensor(out=slope, in0=headm[:, h:h + 1], scalar=SLOPE[h], in1=slope,
                                                  op0=ALU.mult, op1=ALU.add))
                step(dve.memset(sel[:, :], 0.0))
                step(dve.tensor_scalar(sel[:, 56:56 + DS], iot[0:64, 0:DS], q, None, ALU.is_equal))
                dve.wait_ge(sem("ln_in"), 64)
                dve.sem_inc(sem("y_out3"), 16)
                dve.sem_inc(sem("sum_read"), 1)

                for k in range(front_end(P)):
                    dve_front(dve, step, 0, k, P)
                dve_indices(dve, step, 0, P)
                dve_begin(dve, step, P)
                with dve.Fori(0, NT - 1) as t:
                    step.restart()
                    for k in range(NK):
                        dve_expert(dve, t, k, P)
                        dve_front(dve, step, t + 1, k, P)
                        dve_diagonal(dve, t, k, P)
                    dve_indices(dve, step, t + 1, P)
                    dve_sum(dve, step, t, P)
                    dve_begin(dve, step, P)
                    dve_finish(dve, step, t, P)
                step.restart()
                for k in range(NK):
                    dve_expert(dve, NT - 1, k, P)
                    dve_front(dve, step, NT, k, SR)
                    dve_diagonal(dve, NT - 1, k, P)
                for k in range(NK, front_end(SR)):
                    dve_front(dve, step, NT, k, SR)
                dve_indices(dve, step, NT, SR)
                dve_sum(dve, step, NT - 1, P)
                dve_begin(dve, step, SR)
                dve_finish(dve, step, NT - 1, P)
                for k in range(NK):
                    dve_expert(dve, NT, k, SR)
                    if k >= 1:
                        dve_diagonal(dve, NT, k - 1, SR)
                dve_diagonal(dve, NT, NK - 1, SR)
                dve_sum(dve, step, NT, SR)
                dve_finish(dve, step, NT, SR)


_INS = ["x_all", "cache_k", "cache_v", "state_ssm_re", "state_ssm_im", "page_table", "w_in",
        "lambda_q1", "lambda_k1", "lambda_q2", "lambda_k2", "attn_subln_g", "ssm_lambda_re", "ssm_lambda_im",
        "ssm_log_dt", "ssm_b_re", "ssm_b_im", "ssm_c_re", "ssm_c_im", "ssm_d", "ssm_w_glu", "ssm_b_glu",
        "w_out", "ln1_g", "ln1_b", "peer_w_q", "peer_q_g", "peer_sub_keys", "peer_u", "peer_v", "ln2_g", "ln2_b"]
_OUTS = [(1, SEQ, DM), (DB, DS, DM), (1, 1, SEQ, H, 2, DQ), (1, 1, SEQ, H, DV), (1, 1, G, SP_), (1, 1, G, SP_),
         (1, DB, DS, H, 2, DQ), (1, DB, DS, H, DV), (1, DB, G, SP_), (1, DB, G, SP_)]


def kernel(**inputs):
    import numpy as _np
    import concourse.bacc as _bacc
    from concourse import mybir as _mybir
    from concourse.bass_utils import run_bass_kernel_spmd as _run

    nc = _bacc.Bacc("TRN2", target_bir_lowering=False, num_devices=1)
    data = {n: _np.ascontiguousarray(v) for n, v in inputs.items()}
    xp, xs = data.pop("x_prompt"), data.pop("x_sample")
    data["x_all"] = _np.concatenate([xp.reshape(SEQ, DM), xs.reshape(SR, DM), _np.zeros((P - SR, DM), xp.dtype)])
    arrays, ins = {}, {}
    for n in _INS:
        arrays[f"in_{n}"] = data[n]
        ins[n] = nc.dram_tensor(f"in_{n}", data[n].shape, _mybir.dt.from_np(data[n].dtype), kind="ExternalInput").ap()
    outs = [nc.dram_tensor(f"out_{i}", shape, _mybir.dt.float32, kind="ExternalOutput").ap()
            for i, shape in enumerate(_OUTS)]
    build(nc, ins, outs)
    r = _run(nc, [arrays], core_ids=[0])
    return tuple(r.results[0][f"out_{i}"] for i in range(len(_OUTS)))
```
